# Optimizing a Trainium2 kernel written in Bass

```python
import math
import jax, jax.numpy as jnp
from jax import lax
import numpy as np

D_MODEL = 1024
BATCH = 1
SEQ = 1024
DEPTH = 2

CHUNK = 64
N_A_LAYERS = DEPTH // 2
N_B_LAYERS = DEPTH - N_A_LAYERS
POOL_WINDOWS = (2, 4, 8, 16)
N_POOL_GROUPS = len(POOL_WINDOWS)
POOL_GROUP_DIM = D_MODEL // N_POOL_GROUPS
D_FF = -(-8 * D_MODEL // (3 * 256)) * 256
N_HEADS = 8
QK_NOPE_DIM = 128
QK_ROPE_DIM = 64
QK_HEAD_DIM = QK_NOPE_DIM + QK_ROPE_DIM
V_HEAD_DIM = 128
Q_LORA_RANK = 256
KV_LORA_RANK = 512
ROPE_THETA = 10000.0
Q_BLOCK = 128
EPS = 1e-6

kernel_name = "yoco_pool_mla_hybrid"

def rms_norm(x, g):
    xf = x.astype(jnp.float32)
    y = xf * lax.rsqrt(jnp.mean(xf * xf, axis=-1, keepdims=True) + EPS)
    return (y * g.astype(jnp.float32)).astype(x.dtype)

def swiglu(h, w_gate, w_up, w_down):
    return (jax.nn.silu(h @ w_gate) * (h @ w_up)) @ w_down

def pool_mix(h, w_pool, b_pool, scale):
    B, S, D = h.shape
    hf = h.astype(jnp.float32)
    cs0 = jnp.pad(jnp.cumsum(hf, axis=1), ((0, 0), (1, 0), (0, 0)))
    t1 = jnp.arange(1, S + 1)
    groups = []
    for g, w in enumerate(POOL_WINDOWS):
        sl = slice(g * POOL_GROUP_DIM, (g + 1) * POOL_GROUP_DIM)
        c = cs0[:, :, sl]
        lag = jnp.pad(c, ((0, 0), (w, 0), (0, 0)))[:, : S + 1]
        win = (c - lag)[:, 1:]
        cnt = jnp.minimum(t1, w).astype(jnp.float32)[None, :, None]
        groups.append(win / cnt - hf[:, :, sl])
    d = jnp.stack(groups, axis=2).astype(h.dtype)
    y = jnp.einsum('bsgc,gcd->bsgd', d, w_pool) + b_pool
    return y.reshape(B, S, D) * scale

def rope(x, positions):
    R = x.shape[-1]
    half = R // 2
    inv = ROPE_THETA ** (-jnp.arange(half, dtype=jnp.float32) * 2.0 / R)
    ang = positions.astype(jnp.float32)[..., None] * inv
    cos = jnp.cos(ang)[:, :, None, :]
    sin = jnp.sin(ang)[:, :, None, :]
    xf = x.astype(jnp.float32)
    x1, x2 = xf[..., :half], xf[..., half:]
    return jnp.concatenate([x1 * cos - x2 * sin, x2 * cos + x1 * sin], axis=-1).astype(x.dtype)

def shared_kv(h, positions, w_dkv, g_kv_latent, w_uk, w_uv, g_k):
    B, S, _ = h.shape
    ckv = h @ w_dkv
    c = rms_norm(ckv[..., :KV_LORA_RANK], g_kv_latent)
    k_pe = ckv[..., KV_LORA_RANK:]
    k_nope = (c @ w_uk).reshape(B, S, N_HEADS, QK_NOPE_DIM)
    v = (c @ w_uv).reshape(B, S, N_HEADS, V_HEAD_DIM)
    k = jnp.concatenate([k_nope, jnp.broadcast_to(k_pe[:, :, None, :], (B, S, N_HEADS, QK_ROPE_DIM))], axis=-1)
    k = rms_norm(k, g_k)
    k = jnp.concatenate([k[..., :QK_NOPE_DIM], rope(k[..., QK_NOPE_DIM:], positions)], axis=-1)
    return k, v

def mla_queries(h, positions, w_dq, g_q_latent, w_uq, g_q):
    B, S, _ = h.shape
    cq = rms_norm(h @ w_dq, g_q_latent)
    q = (cq @ w_uq).reshape(B, S, N_HEADS, QK_HEAD_DIM)
    q = rms_norm(q, g_q)
    return jnp.concatenate([q[..., :QK_NOPE_DIM], rope(q[..., QK_NOPE_DIM:], positions)], axis=-1)

def chunk_causal_attention(q, k, v):
    S = q.shape[1]
    scale = 1.0 / math.sqrt(QK_HEAD_DIM)
    outs = []
    for i in range(S // Q_BLOCK):
        start, end = i * Q_BLOCK, (i + 1) * Q_BLOCK
        s = jnp.einsum('bqhd,bkhd->bhqk', q[:, start:end], k[:, :end]).astype(jnp.float32) * scale
        qc = (start + jnp.arange(Q_BLOCK)) // CHUNK
        kc = jnp.arange(end) // CHUNK
        mask = kc[None, :] <= qc[:, None]
        s = jnp.where(mask[None, None], s, jnp.float32(-1e30))
        p = jax.nn.softmax(s, axis=-1).astype(v.dtype)
        outs.append(jnp.einsum('bhqk,bkhd->bqhd', p, v[:, :end]))
    return jnp.concatenate(outs, axis=1)

def setup_inputs(seed: int = 0) -> dict:
    key = jax.random.key(seed)
    ks = iter(jax.random.split(key, 32))
    f32 = jnp.float32

    def w(shape, fan_in):
        return jax.random.normal(next(ks), shape, f32) * fan_in ** -0.5

    def gain(shape):
        return 1.0 + 0.02 * jax.random.normal(next(ks), shape, f32)

    x = jax.random.normal(next(ks), (BATCH, SEQ, D_MODEL), f32)
    positions = jnp.broadcast_to(jnp.arange(SEQ, dtype=jnp.int32)[None, :], (BATCH, SEQ)).astype(jnp.int32)
    return {
        "x": x,
        "positions": positions,
        "ln_mix_a": gain((N_A_LAYERS, D_MODEL)),
        "w_pool": w((N_A_LAYERS, N_POOL_GROUPS, POOL_GROUP_DIM, POOL_GROUP_DIM), POOL_GROUP_DIM),
        "b_pool": 0.02 * jax.random.normal(next(ks), (N_A_LAYERS, N_POOL_GROUPS, POOL_GROUP_DIM), f32),
        "pool_scale": gain((N_A_LAYERS, D_MODEL)),
        "ln_ffn": gain((DEPTH, D_MODEL)),
        "w_gate": w((DEPTH, D_MODEL, D_FF), D_MODEL),
        "w_up": w((DEPTH, D_MODEL, D_FF), D_MODEL),
        "w_down": w((DEPTH, D_FF, D_MODEL), D_FF),
        "ln_kv": gain((D_MODEL,)),
        "w_dkv": w((D_MODEL, KV_LORA_RANK + QK_ROPE_DIM), D_MODEL),
        "g_kv_latent": gain((KV_LORA_RANK,)),
        "w_uk": w((KV_LORA_RANK, N_HEADS * QK_NOPE_DIM), KV_LORA_RANK),
        "w_uv": w((KV_LORA_RANK, N_HEADS * V_HEAD_DIM), KV_LORA_RANK),
        "g_k": gain((QK_HEAD_DIM,)),
        "ln_mix_b": gain((N_B_LAYERS, D_MODEL)),
        "w_dq": w((N_B_LAYERS, D_MODEL, Q_LORA_RANK), D_MODEL),
        "g_q_latent": gain((N_B_LAYERS, Q_LORA_RANK)),
        "w_uq": w((N_B_LAYERS, Q_LORA_RANK, N_HEADS * QK_HEAD_DIM), Q_LORA_RANK),
        "g_q": gain((N_B_LAYERS, QK_HEAD_DIM)),
        "w_o": w((N_B_LAYERS, N_HEADS * V_HEAD_DIM, D_MODEL), N_HEADS * V_HEAD_DIM),
    }

def reference(x, positions, ln_mix_a, w_pool, b_pool, pool_scale, ln_ffn, w_gate, w_up, w_down,
              ln_kv, w_dkv, g_kv_latent, w_uk, w_uv, g_k,
              ln_mix_b, w_dq, g_q_latent, w_uq, g_q, w_o):
    B, S, D = x.shape
    k_sh, v_sh = None, None
    for l in range(DEPTH):
        if l < N_A_LAYERS:
            x = x + pool_mix(rms_norm(x, ln_mix_a[l]), w_pool[l], b_pool[l], pool_scale[l])
        else:
            j = l - N_A_LAYERS
            q = mla_queries(rms_norm(x, ln_mix_b[j]), positions, w_dq[j], g_q_latent[j], w_uq[j], g_q[j])
            o = chunk_causal_attention(q, k_sh, v_sh)
            x = x + o.reshape(B, S, N_HEADS * V_HEAD_DIM) @ w_o[j]
        x = x + swiglu(rms_norm(x, ln_ffn[l]), w_gate[l], w_up[l], w_down[l])
        if l == N_A_LAYERS - 1:
            k_sh, v_sh = shared_kv(rms_norm(x, ln_kv), positions, w_dkv, g_kv_latent, w_uk, w_uv, g_k)
    return x


_drawn_inputs = setup_inputs


def setup_inputs(seed=0):
    import zlib

    import numpy as np

    out = dict(_drawn_inputs(seed))
    spreads = {}
    factors = {'ln_mix_a': 3.427,
     'b_pool': 3.032,
     'pool_scale': 3.71,
     'ln_ffn': 3.262,
     'ln_kv': 8.0,
     'g_kv_latent': 8.0,
     'g_k': 8.0,
     'ln_mix_b': 8.0,
     'g_q_latent': 8.0,
     'g_q': 8.0}
    for name, (base, spread) in spreads.items():
        noise = np.random.default_rng([zlib.crc32(name.encode()), seed]).standard_normal(out[name].shape)
        drawn = base * np.exp(spread * noise) if base else spread * noise
        out[name] = __import__('jax').numpy.asarray(drawn.astype(out[name].dtype))
    for name, factor in factors.items():
        out[name] = (out[name] * factor).astype(out[name].dtype)
    return out
```

```python
import math

import numpy as np
import concourse.bass as bass
from concourse import mybir
from contextlib import ExitStack

STAGE = 9


def build_trunk(nc, a, out, stage=9):
    F = mybir.dt.float32
    R = mybir.dt.float32r
    ALU = mybir.AluOpType
    ACT = mybir.ActivationFunctionType
    AX = mybir.AxisListType

    P = 128
    T, D = a["x"].shape[1:]
    FF = a["w_gate"].shape[2]
    KD = D // P
    NT = T // P
    HT = 512
    NF = FF // P
    NG = NF // 2
    NCH = 2 * KD
    EPS = 1e-6
    WINDOWS = (2, 4, 8, 16)
    KB = 1024
    BASE = 16512
    RL = a["w_dkv"].shape[1]
    KVR = a["g_kv_latent"].shape[0]
    QR = a["g_q_latent"].shape[1]
    ROPE = RL - KVR
    HR = ROPE // 2
    QKD = a["g_k"].shape[0]
    NOPE = QKD - ROPE
    NH = a["w_uq"].shape[2] // QKD
    KC, KQ = KVR // P, QR // P
    CW = RL + QR
    SCALE = 1.0 / math.sqrt(QKD)
    CHUNK = 64
    NEG = -1e30
    TWO_PI = 2.0 * math.pi
    MAGIC = 1.5 * 2.0 ** 23
    inv_freq = np.power(np.float32(10000.0), -np.arange(HR, dtype=np.float32) * np.float32(2.0) / np.float32(ROPE))

    def pieces(v, n):
        got = []
        for _ in range(n):
            e = math.floor(math.log2(abs(v)))
            q = 2.0 ** (e - 11)
            got.append(math.floor(v / q) * q)
            v -= got[-1]
        return got

    ctx = ExitStack()
    with ctx:
        def at(name, shape, dt, offset):
            return nc.alloc_sbuf_tensor_at(name, shape, dt, offset=BASE + int(offset))

        def sem(name):
            return ctx.enter_context(nc.semaphore(name))

        xT = at("xT", [P, KD, T], F, 0)
        hi_x = at("hi_x", [P, KD, T], R, 32 * KB)
        lo_x = at("lo_x", [P, KD, T], R, 64 * KB)
        gu_hi = at("gu_hi", [P, 2, 2 * KD, P], R, 96 * KB)
        gu_lo = at("gu_lo", [P, 2, 2 * KD, P], R, 112 * KB)
        a_hi = at("a_hi", [P, 2, 2, T], R, 128 * KB)
        a_lo = at("a_lo", [P, 2, 2, T], R, 144 * KB)
        wd_hi = at("wd_hi", [P, 2, D], R, 160 * KB)
        wd_lo = at("wd_lo", [P, 2, D], R, 168 * KB)
        raw_gu = at("raw_gu", [P, 2 * KD, 2 * P], F, 176 * KB)
        raw_wd = at("raw_wd", [P, D], F, 192 * KB)
        sil = at("sil", [P, 2, HT], F, 196 * KB)
        a32 = at("a32", [P, 2, HT], F, 200 * KB)
        sq = at("sq", [P, 2, HT], F, 196 * KB)
        diag = at("diag", [P, 4, P], F, 200 * KB)
        CB = 204 * KB
        ident = at("ident", [P, P], F, CB)
        ones = at("ones", [P, P], F, CB + 512)
        NROW = 64
        gT = at("gT", [P, NROW], F, CB + 1024)
        ss = at("ss", [P, NT], F, CB + 1280)
        rms = at("rms", [P, NT], F, CB + 1312)
        nhalf = at("nhalf", [P, 16], F, CB + 1344)
        bs = at("bs", [P, KD], F, CB + 1408)
        xtok = at("xtok", [P, NT, D], F, 128 * KB)
        hp = at("hp", [P, 2, 2, T], F, 96 * KB)
        sA = at("sA", [P, 2, T], F, 112 * KB)
        sB = at("sB", [P, 2, T], F, 120 * KB)
        wp_raw = at("wp_raw", [P, 2 * len(WINDOWS), 2 * P], F, 192 * KB)
        wp_hi = at("wp_hi", [P, 2 * len(WINDOWS), 2 * P], R, 160 * KB)
        wp_lo = at("wp_lo", [P, 2 * len(WINDOWS), 2 * P], R, 168 * KB)
        grow = at("grow", [NROW, P], F, 200 * KB)
        invc = at("invc", [P, 16], F, 200 * KB + 512)
        edge = at("edge", [P, 2, 16], F, 200 * KB + 576)
        sqt = at("sqt", [P, D], F, 176 * KB)
        diagA = at("diagA", [P, NT, P], F, 180 * KB)
        ytmp = at("ytmp", [P, 2, HT], F, 184 * KB)

        cos_t = at("cos_t", [P, NT, HR], F, CB + 1536)
        sin_t = at("sin_t", [P, NT, HR], F, CB + 2560)
        tab = at("tab", [P, 6, NT, HR], F, 32 * KB)
        pos_i = at("pos_i", [NT, P], mybir.dt.int32, 41 * KB)
        pos_row = at("pos_row", [NT, P], F, 42 * KB)
        pos_f = at("pos_f", [P, NT], F, 40 * KB + 64)
        inv_t = at("inv_t", [P, HR], F, 40 * KB + 128)
        halfpi = at("halfpi", [P, 1], F, 40 * KB + 256)
        wc_hi = at("wc_hi", [P, KD, CW], R, 96 * KB)
        wc_lo = at("wc_lo", [P, KD, CW], R, 128 * KB)
        raw_c = at("raw_c", [P, 4, CW], F, 176 * KB)
        junk = at("junk", [P, CW], F, 122 * KB)
        c_tok = at("c_tok", [P, 2, KVR + QR], F, 154 * KB)
        cT_hi = at("cT_hi", [P, KC, T], R, 0)
        cT_lo = at("cT_lo", [P, KC, T], R, 16 * KB)
        cqT_hi = at("cqT_hi", [P, KQ, T], R, 160 * KB)
        cqT_lo = at("cqT_lo", [P, KQ, T], R, 168 * KB)
        kpe = at("kpe", [P, NT, ROPE], F, 200 * KB)
        g_rope = at("g_rope", [P, 2, ROPE], F, 202 * KB)
        ssl = at("ssl", [P, NT, 2], F, 202 * KB + 512)
        rl = at("rl", [P, NT, 2], F, 202 * KB + 576)
        ssqpe = at("ssqpe", [P, NH, NT], F, 202 * KB + 640)
        sskpe = at("sskpe", [P, NT], F, CB + 3840)
        gkq = at("gkq", [P, 1], F, CB + 3872)
        kn = at("kn", [P, NH, T], F, 32 * KB)
        qn = at("qn", [P, NH, T], F, 64 * KB)
        v32 = at("v32", [P, NT, NH * P], F, 96 * KB)
        qpe = at("qpe", [P, NT, NH, ROPE], F, 128 * KB)
        krT = at("krT", [P, T], F, 144 * KB)
        krd = at("krd", [P, NT, 2, ROPE], F, 148 * KB)
        kg = at("kg", [P, NT, ROPE], F, 32 * KB)
        krt = at("krt", [P, 2, NT, HR], F, 34 * KB)
        dsq = at("dsq", [P, 2, HT], F, 148 * KB)
        rt = at("rt", [P, 4, 2, 4, HR], F, 152 * KB)
        qsq = at("qsq", [P, 2, 4, ROPE], F, 156 * KB)
        qg = at("qg", [P, 2, 4, ROPE], F, 158 * KB)
        dw_raw = at("dw_raw", [P, 2, 4, 2 * P], F, 176 * KB)
        dw_hi = at("dw_hi", [P, 2, 4, 2 * P], R, 184 * KB)
        dw_lo = at("dw_lo", [P, 2, 4, 2 * P], R, 192 * KB)
        rk = at("rk", [P, NH, NT], F, CB + 3584)
        rq = at("rq", [P, NH, NT], F, CB + 1536)
        nrq = at("nrq", [P, NH, NT], F, CB + 1792)
        mx = at("mx", [P, 2], F, CB + 2048)
        nb = at("nb", [P, 2], F, CB + 2080)
        esum = at("esum", [P, 2], F, CB + 2112)
        rsum = at("rsum", [P, 2], F, CB + 2144)
        khi = at("khi", [P, 2, T], R, 0)
        klo = at("klo", [P, NH, T], R, 32 * KB)
        kr1 = at("kr1", [P, 2, T], R, 8 * KB)
        kr2 = at("kr2", [P, 2, T], R, 16 * KB)
        qs = at("qs", [P, 2, T], R, 24 * KB)
        qhi = at("qhi", [P, 2, T], R, 148 * KB)
        qlo = at("qlo", [P, 2, T], R, 156 * KB)
        v_hi = at("v_hi", [P, NT, P], R, 164 * KB)
        v_lo = at("v_lo", [P, NT, P], R, 168 * KB)
        pt_hi = at("pt_hi", [P, NT, 2 * P], R, 172 * KB)
        pt_lo = at("pt_lo", [P, NT, 2 * P], R, 180 * KB)
        e32 = at("e32", [P, 2, T], F, 188 * KB)
        kdiag = at("kdiag", [P, 4, P], F, 196 * KB)
        krs = at("krs", [P, HT], F, 198 * KB)
        qhl = at("qhl", [P, NT, 2, ROPE], R, 200 * KB)
        wo_raw = at("wo_raw", [P, 2, NH, 2 * P], F, 128 * KB)
        wo_hi = at("wo_hi", [P, 2, NH, 2 * P], R, 96 * KB)
        wo_lo = at("wo_lo", [P, 2, NH, 2 * P], R, 112 * KB)

        PS = ctx.enter_context(nc.psum_tensor("banks", [P, 8, 512], F))
        ps = [PS[:, i, :] for i in range(8)]
        ps_scores = [PS[:, 2 * i:2 * i + 2, :].rearrange("p b c -> p (b c)") for i in range(2)]

        ROW = {}
        at_row = 0
        for name, n in (("ln_mix_a", 8), ("pool_scale", 8), ("b_pool", 8), ("ln_ffn0", 8), ("ln_ffn1", 8),
                        ("ln_kv", 8), ("ln_mix_b", 8), ("g_kv_latent", 4), ("g_q_latent", 2), ("g_k", 1), ("g_q", 1)):
            ROW[name] = at_row
            at_row += n
        assert at_row == NROW

        def gain(name, k):
            return gT[:, ROW[name] + k:ROW[name] + k + 1]

        g_src = [("ln_mix_a", a["ln_mix_a"][0, :], 8), ("pool_scale", a["pool_scale"][0, :], 8),
                 ("b_pool", a["b_pool"][0, :, :].rearrange("g c -> (g c)"), 8),
                 ("ln_ffn0", a["ln_ffn"][0, :], 8), ("ln_ffn1", a["ln_ffn"][1, :], 8), ("ln_kv", a["ln_kv"], 8),
                 ("ln_mix_b", a["ln_mix_b"][0, :], 8), ("g_kv_latent", a["g_kv_latent"], 4),
                 ("g_q_latent", a["g_q_latent"][0, :], 2), ("g_k", a["g_k"][0:P], 1), ("g_q", a["g_q"][0, 0:P], 1)]

        s_x = [sem(f"x_in{t}") for t in range(NT)]
        s_g = sem("gains_in")
        s_wp = sem("w_pool_in")
        s_const = sem("constants")
        s_gT = sem("gains_transposed")
        s_gc = sem("gains_copied")
        s_bs = sem("bias_scaled")
        s_xtr = sem("x_transposed")
        s_xev = sem("x_evacuated")
        s_ssA = sem("square_sums_a")
        s_pool1 = sem("pool_steps")
        s_rA = sem("rms_a")
        s_dgA = sem("diag_a")
        s_bcA = sem("rms_broadcast_a")
        s_dve = sem("vector_steps")
        s_h = sem("pool_h")
        s_win = sem("window_sums")
        s_d32 = sem("pool_d")
        s_dhi = sem("pool_d_hi")
        s_dlo = sem("pool_d_lo")
        s_wph = sem("w_pool_hi")
        s_wpl = sem("w_pool_lo")
        s_py = sem("pool_y")
        s_rgu = sem("gate_up_in")
        s_rwd = sem("down_in")
        s_guh = sem("gate_up_hi")
        s_gul = sem("gate_up_lo")
        s_wdh = sem("down_hi")
        s_wdl = sem("down_lo")
        s_gumm = sem("gate_up_products")
        s_sil = sem("silu_done")
        s_a32 = sem("a_done")
        s_ahi = sem("a_hi_done")
        s_alo = sem("a_lo_done")
        s_dmm = sem("residual_products")
        s_xadd = sem("x_added")
        s_sq = sem("squares")
        s_ssm = sem("square_sum_products")
        s_ss = sem("square_sums")
        s_r = sem("rms")
        s_dg = sem("diag")
        s_bc = sem("rms_broadcast")
        s_h32 = sem("h_done")
        s_hhi = sem("h_hi_done")
        s_hlo = sem("h_lo_done")
        s_pos = sem("positions_in")
        s_posf = sem("positions_float")
        s_posT = sem("positions_transposed")
        s_ang = sem("angles_reduced")
        s_tab = sem("rope_tables")
        s_spill = sem("x_spilled")
        s_cr = [sem(f"latent_weights_in{i}") for i in range(4)]
        s_gr = sem("rope_gains_in")
        s_wch = sem("latent_weights_hi")
        s_wcl = sem("latent_weights_lo")
        s_xch = sem("x_hi_latent")
        s_xcl = sem("x_lo_latent")
        s_cmm = sem("latent_products")
        s_csq = sem("latent_square_sums")
        s_rl = sem("latent_rms")
        s_ctok = sem("latents_normed")
        s_ctr = sem("latents_transposed")
        s_chi = sem("latents_hi")
        s_clo = sem("latents_lo")
        s_krd = sem("key_part_rotated")
        s_krtr = sem("key_part_transposed")
        s_krT = sem("key_part_ready")
        s_dwr = [sem(f"head_weights_in{i}") for i in range(2)]
        s_dwh = sem("head_weights_hi")
        s_dwl = sem("head_weights_lo")
        s_vmm = sem("value_products")
        s_vev = sem("values_evacuated")
        s_kmm = sem("head_products")
        s_kev = sem("heads_evacuated")
        s_ksq = sem("head_squares")
        s_kst = sem("head_square_sums")
        s_kstc = sem("head_sums_copied")
        s_rk = sem("head_rms")
        s_qrmm = sem("query_part_products")
        s_qsq = sem("query_part_squares")
        s_qg = sem("query_part_gained")
        s_qcs = sem("query_part_crossed")
        s_qpe = sem("query_part_rotated")
        s_rqs = sem("query_scales")
        s_kd = sem("key_rms_diag")
        s_kbc = sem("key_rms_broadcast")
        s_kf = sem("keys_scaled")
        s_khi = sem("keys_hi")
        s_klo = sem("keys_lo")
        s_qh = sem("queries_hi")
        s_ql = sem("queries_lo")
        s_qhl = sem("query_part_split")
        s_qtr = sem("query_part_transposed")
        s_qs = sem("query_part_ready")
        s_vh = sem("values_hi")
        s_vl = sem("values_lo")
        s_sc = sem("scores")
        s_mask = sem("scores_masked")
        s_max = sem("row_maxima")
        s_nb = sem("exp_biases")
        s_exp = sem("exponentials")
        s_rs = sem("row_sums_inverted")
        s_p = sem("probabilities")
        s_ptr = sem("probabilities_transposed")
        s_pth = sem("probabilities_hi")
        s_ptl = sem("probabilities_lo")
        s_pv = sem("attention_products")
        s_o = sem("attention_out")
        s_back = sem("x_back")
        s_wor = [sem(f"w_o_in{i}") for i in range(2)]
        s_woh = sem("w_o_hi")
        s_wol = sem("w_o_lo")
        s_oh = sem("o_hi")
        s_ol = sem("o_lo")
        s_omm = sem("w_o_products")
        s_ox = sem("x_attention_added")
        s_otr = sem("out_transposed")
        s_oev = sem("out_first_half")
        s_oev2 = sem("out_second_half")
        s_out = sem("out_written")

        x_in = a["x"][0, :, :].rearrange("(t p) d -> t p d", p=P)
        x_out = out[0, :, :].rearrange("(t p) d -> t p d", p=P)
        wdkv_v = a["w_dkv"].rearrange("(k p) c -> p k c", p=P)
        wdq_v = a["w_dq"][0, :, :].rearrange("(k p) c -> p k c", p=P)
        wuk_v = a["w_uk"].rearrange("(k p) c -> p k c", p=P)
        wuv_v = a["w_uv"].rearrange("(k p) c -> p k c", p=P)
        wuq_v = a["w_uq"][0, :, :].rearrange("(k p) (h c) -> p k h c", p=P, c=QKD)
        wo_v = a["w_o"][0, :, :].rearrange("(k p) c -> p k c", p=P)
        x_mid = nc.dram_tensor("x_mid", (P, KD, T), F, kind="Internal").ap()
        wg_v = [a["w_gate"][l, :, :].rearrange("(k p) f -> p k f", p=P) for l in range(2)]
        wu_v = [a["w_up"][l, :, :].rearrange("(k p) f -> p k f", p=P) for l in range(2)]
        wd_v = [a["w_down"][l, :, :].rearrange("(f p) d -> f p d", p=P) for l in range(2)]

        NCONST = 20 + HR
        TR = [sum(i // 4 + 1 for i in range(m + 1)) for m in range(NT)]

        def table(t, n):
            return t[:, 2 * n:2 * n + 2, :].unsqueeze(2).broadcast_to([P, 2, 4, HR])

        def half(h):
            return slice(h * HT, (h + 1) * HT)

        block = ctx.enter_context(nc.Block())

        @block.sync
        def _(sp):
            sp.dma_start(pos_i[:, :], a["positions"][0, :].rearrange("(t p) -> t p", p=P)).then_inc(s_pos, 16)
            for t in range(NT):
                sp.dma_start(xtok[:, t, :], x_in[t, :, :]).then_inc(s_x[t], 16)
                if t == 1:
                    for name, src, n in g_src:
                        sp.dma_start(grow[ROW[name]:ROW[name] + n, :], src.rearrange("(k p) -> k p", p=P)).then_inc(s_g, 16)
                    sp.dma_start(wp_raw[:, :, :], a["w_pool"][0, :, :, :].rearrange("g (k p) d -> p (g k) d", p=P)).then_inc(s_wp, 16)

            def load_gate_up(l, i):
                g = l * NG + i
                if not (isinstance(g, int) and g == 0):
                    sp.wait_ge(s_gul, 2 * g)
                sp.dma_start(raw_gu[:, 0:KD, :], wg_v[l][:, :, bass.ds(i * 2 * P, 2 * P)]).then_inc(s_rgu, 16)
                sp.dma_start(raw_gu[:, KD:2 * KD, :], wu_v[l][:, :, bass.ds(i * 2 * P, 2 * P)]).then_inc(s_rgu, 16)

            def load_down(l, f):
                n = l * NF + f
                if not (isinstance(n, int) and n == 0):
                    sp.wait_ge(s_wdl, n)
                sp.dma_start(raw_wd[:, :], wd_v[l][f, :, :]).then_inc(s_rwd, 16)

            def ffn(l):
                load_gate_up(l, 0)
                load_down(l, 0)
                load_gate_up(l, 1)
                for i in range(NG - 2):
                    load_down(l, 2 * i + 1)
                    load_gate_up(l, i + 2)
                    load_down(l, 2 * i + 2)
                load_down(l, NF - 3)
                load_down(l, NF - 2)
                load_down(l, NF - 1)

            sp.wait_ge(s_dmm, 16)
            sp.wait_ge(s_xadd, 16)
            ffn(0)
            if stage >= 3:
                sp.wait_ge(s_gul, NF)
                for k in range(KD):
                    if k >= 4:
                        sp.wait_ge(s_wcl, k - 3)
                    sp.dma_start(raw_c[:, k % 4, 0:RL], wdkv_v[:, k, :]).then_inc(s_cr[k % 4], 16)
                    sp.dma_start(raw_c[:, k % 4, RL:CW], wdq_v[:, k, :]).then_inc(s_cr[k % 4], 16)
                    if k == 3:
                        sp.wait_ge(s_xadd, NCH * (NG + 1) - KD)
                        sp.dma_start(x_mid[:, :, 0:HT], xT[:, :, 0:HT]).then_inc(s_spill, 16)
                        sp.dma_start(g_rope[:, 0, :], a["g_k"][NOPE:QKD].partition_broadcast(P)).then_inc(s_gr, 16)
                        sp.dma_start(g_rope[:, 1, :], a["g_q"][0, NOPE:QKD].partition_broadcast(P)).then_inc(s_gr, 16)
                        sp.wait_ge(s_xadd, NCH * (NG + 1))
                        sp.dma_start(x_mid[:, :, HT:T], xT[:, :, HT:T]).then_inc(s_spill, 16)
                sp.wait_ge(s_wcl, KD)
                for u in range(14):
                    if u >= 2:
                        sp.wait_ge(s_dwl, u - 1)
                    raw, done = dw_raw[:, u % 2, :, :], s_dwr[u % 2]
                    if u < 4:
                        sp.dma_start(raw, wuv_v[:, :, 2 * P * u:2 * P * (u + 1)]).then_inc(done, 16)
                    elif u < 8:
                        sp.dma_start(raw, wuk_v[:, :, 2 * P * (u - 4):2 * P * (u - 3)]).then_inc(done, 16)
                    else:
                        for k in range(KQ):
                            if u < 10:
                                n = u - 8
                                sp.dma_start(raw[:, k, :].rearrange("p (h c) -> p h c", c=ROPE),
                                             wuq_v[:, k, 4 * n:4 * n + 4, NOPE:QKD]).then_inc(done, 16)
                            else:
                                n = u - 10
                                sp.dma_start(raw[:, k, :].rearrange("p (h c) -> p h c", c=NOPE),
                                             wuq_v[:, k, 2 * n:2 * n + 2, 0:NOPE]).then_inc(done, 16)
                sp.wait_ge(s_qtr, 2 * NH)
                sp.wait_ge(s_qs, 2 * NH)
                for u in range(4):
                    if u >= 2:
                        sp.wait_ge(s_wol, u - 1)
                    sp.dma_start(wo_raw[:, u % 2, :, :], wo_v[:, :, 2 * P * u:2 * P * (u + 1)]).then_inc(s_wor[u % 2], 16)
                    if u == 1:
                        sp.wait_ge(s_sc, NH * NT)
                        sp.wait_ge(s_spill, 32)
                        for k in range(2):
                            sp.dma_start(xT[:, 4 * k:4 * k + 4, :], x_mid[:, 4 * k:4 * k + 4, :]).then_inc(s_back, 16)
                sp.wait_ge(s_pv, 4 * NH)
                sp.wait_ge(s_ptl, 12 * NH)
                sp.wait_ge(s_p, NH * NT)
            if stage >= 2:
                ffn(1)
            for t in range(NT):
                sp.wait_ge(s_oev, t + 1)
                sp.wait_ge(s_oev2, t + 1)
                sp.dma_start(x_out[t, :, :], xtok[:, t, :]).then_inc(s_out, 16)
            sp.wait_ge(s_out, 16 * NT)

        @block.gpsimd
        def _(pool):
            steps1 = [0]

            def link(ins):
                steps1[0] += 1
                ins.then_inc(s_pool1, 1)
                pool.wait_ge(s_pool1, steps1[0])

            link(pool.memset(ident[:, :], 0.0))
            pool.affine_select(out=ident[:, :], in_=ident[:, :], compare_op=ALU.not_equal, fill=1.0, base=0,
                               pattern=[[-1, P]], channel_multiplier=1).then_inc(s_const, 1)
            pool.memset(ones[:, :], 1.0).then_inc(s_const, 1)
            pool.memset(nhalf[:, :], -0.5).then_inc(s_const, 1)
            for j in range(16):
                pool.memset(invc[:, j:j + 1], 1.0 / (j + 1)).then_inc(s_const, 1)
            for j in range(HR):
                pool.memset(inv_t[:, j:j + 1], float(inv_freq[j])).then_inc(s_const, 1)
            pool.memset(halfpi[:, :], math.pi / 2).then_inc(s_const, 1)
            pool.wait_ge(s_const, NCONST)

            for t in range(NT):
                pool.wait_ge(s_ssA, t + 1)
                link(pool.tensor_scalar(rms[:, t:t + 1], ss[:, t:t + 1], 1.0 / D, EPS, ALU.mult, ALU.add))
                pool.tensor_tensor(rms[:, t:t + 1], rms[:, t:t + 1], nhalf[:, 0:1], ALU.pow).then_inc(s_rA, 1)
            steps = 0
            for g, w in enumerate(WINDOWS):
                src = hp[:, g % 2, :, :]
                pool.wait_ge(s_h, g + 1)
                if g >= 1:
                    pool.wait_ge(s_d32, g)
                sh = 1
                bufs = [sA, sB]
                n = 0
                while sh < w:
                    dst = bufs[n % 2][:, :, :]
                    pool.tensor_copy(dst[:, :, 0:sh], src[:, :, 0:sh]).then_inc(s_win, 1)
                    pool.tensor_tensor(dst[:, :, sh:T], src[:, :, sh:T], src[:, :, 0:T - sh], ALU.add).then_inc(s_win, 1)
                    steps += 2
                    pool.wait_ge(s_win, steps)
                    src = dst
                    sh *= 2
                    n += 1

            def stats(q, h):
                pool.wait_ge(s_ss, 2 * q + h + 1)
                part = rms[:, 4 * h:4 * h + 4]
                link(pool.tensor_scalar(part, ss[:, 4 * h:4 * h + 4], 1.0 / D, EPS, ALU.mult, ALU.add))
                pool.tensor_tensor(part, part, nhalf[:, 0:4], ALU.pow).then_inc(s_r, 1)

            stats(0, 0)
            stats(0, 1)
            if stage == 2:
                stats(1, 0)
                stats(1, 1)
            if stage < 3:
                return

            for h in range(2):
                for k in range(KD):
                    pool.wait_ge(s_xch, KD * h + k + 1)
                    pool.tensor_tensor(lo_x[:, k, half(h)], xT[:, k, half(h)], hi_x[:, k, half(h)].bitcast(F),
                                       ALU.subtract).then_inc(s_xcl, 1)
                stats(1, h)
            for t in range(NT):
                pool.wait_ge(s_csq, t + 1)
                pool.tensor_scalar(rl[:, t, 0:1], ssl[:, t, 0:1], 1.0 / KVR, EPS, ALU.mult, ALU.add)
                link(pool.tensor_scalar(rl[:, t, 1:2], ssl[:, t, 1:2], 1.0 / QR, EPS, ALU.mult, ALU.add))
                pool.tensor_tensor(rl[:, t, :], rl[:, t, :], nhalf[:, 0:2], ALU.pow).then_inc(s_rl, 1)

            def head_rms(p):
                pool.wait_ge(s_kstc, p + 1)
                r = (rk, rq)[p // 4][:, 2 * (p % 4):2 * (p % 4) + 2, :].rearrange("p h t -> p (h t)")
                link(pool.tensor_scalar(r, r, 1.0 / QKD, EPS, ALU.mult, ALU.add))
                pool.tensor_tensor(r, r, nhalf[:, :], ALU.pow).then_inc(s_rk, 1)

            for p in range(4):
                head_rms(p)
            for n in range(8):
                pool.wait_ge(s_qg, n + 1)
                if n >= 1:
                    pool.wait_ge(s_qpe, n)
                pool.tensor_tensor(rt[:, 2, :, :, :], qg[:, :, :, HR:ROPE], table(cos_t, n % 4), ALU.mult)
                pool.tensor_tensor(rt[:, 3, :, :, :], qg[:, :, :, 0:HR], table(sin_t, n % 4), ALU.mult).then_inc(s_qcs, 1)
            for p in range(4, 8):
                head_rms(p)

            def query_part(h):
                pool.wait_ge(s_qh, h + 1)
                pool.tensor_tensor(qhl[:, :, 1, :], qpe[:, :, h, :], qhl[:, :, 0, :].bitcast(F),
                                   ALU.subtract).then_inc(s_qhl, 1)

            def values(h):
                pool.wait_ge(s_vh, h + 1)
                pool.tensor_tensor(v_lo[:, :, :], v32[:, :, bass.ds(h * P, P)], v_hi[:, :, :].bitcast(F),
                                   ALU.subtract).then_inc(s_vl, 1)

            def keys_and_queries(h, u):
                for f in range(2):
                    pool.wait_ge(s_khi, 2 * h + f + 1)
                    pool.tensor_tensor(klo[:, h, half(f)], kn[:, h, half(f)], khi[:, u, half(f)].bitcast(F), ALU.subtract)
                    pool.tensor_tensor(kr2[:, u, half(f)], krs[:, :], kr1[:, u, half(f)].bitcast(F),
                                       ALU.subtract).then_inc(s_klo, 1)
                pool.tensor_tensor(qlo[:, u, :], qn[:, h, :], qhi[:, u, :].bitcast(F), ALU.subtract).then_inc(s_ql, 1)

            query_part(0)
            keys_and_queries(0, 0)
            values(0)
            query_part(1)
            keys_and_queries(1, 1)
            with pool.Fori(0, 3) as j:
                for w in range(2):
                    h = 2 * j + 1 + w
                    query_part(h + 1)
                    values(h)
                    keys_and_queries(h + 1, w)
            values(NH - 1)
            stats(2, 0)
            stats(2, 1)

        @block.scalar
        def _(act):
            for t in range(NT):
                act.wait_ge(s_x[t], 16)
                if t >= 1:
                    act.wait_ge(s_ssA, t)
                act.activation(sqt[:, :], xtok[:, t, :], ACT.Square, accum_out=ss[:, t:t + 1]).then_inc(s_ssA, 1)
            act.wait_ge(s_ang, 1)
            act.wait_ge(s_const, NCONST)
            act.activation(sin_t[:, :, :], tab[:, 4, :, :], ACT.Sin)
            act.activation(cos_t[:, :, :], tab[:, 5, :, :], ACT.Sin, scale=-1.0, bias=halfpi[:, 0:1]).then_inc(s_tab, 1)
            act.wait_ge(s_wp, 16)
            act.activation(wp_hi[:, :, :], wp_raw[:, :, :], ACT.Copy).then_inc(s_wph, 1)
            act.wait_ge(s_bs, 1)

            def pool_y(n):
                g, dt, h = n // 4, (n // 2) % 2, n % 2
                k = 2 * g + dt
                act.wait_ge(s_dmm, n + 1)
                if n >= 2:
                    act.wait_ge(s_xadd, n - 1)
                act.activation(ytmp[:, n % 2, :], ps[4 + n % 4][:, :], ACT.Identity, scale=gain("pool_scale", k),
                               bias=bs[:, k:k + 1]).then_inc(s_py, 1)

            for g in range(4):
                act.wait_ge(s_d32, g + 1)
                act.activation(hi_x[:, 2 * g:2 * g + 2, :], hp[:, g % 2, :, :], ACT.Copy).then_inc(s_dhi, 1)
                if g >= 1:
                    for n in range(4 * g - 4, 4 * g):
                        pool_y(n)
            for n in range(12, 16):
                pool_y(n)

            def squares(q, h, wait_x):
                for k in range(KD):
                    n = (2 * q + h) * KD + k
                    wait_x(act, h)
                    if n >= 2:
                        act.wait_ge(s_ssm, n - 1)
                    act.activation(sq[:, k % 2, :], xT[:, k, half(h)], ACT.Square).then_inc(s_sq, 1)

            def norm(q, l, wait_x):
                for h in range(2):
                    squares(q, h, wait_x)
                for h in range(2):
                    for k in range(KD):
                        n = (2 * l + h) * KD + k
                        act.wait_ge(s_h32, n + 1)
                        act.activation(hi_x[:, k, half(h)], sq[:, k % 2, :], ACT.Copy).then_inc(s_hhi, 1)

            def split_gate_up(l, i, u):
                g, n = l * NG + i, l * NF + 2 * i + u
                if u == 0:
                    act.wait_ge(s_rgu, 32 * g + 32)
                if not (isinstance(n, int) and n < 2):
                    act.wait_ge(s_gumm, 2 * n - 2)
                act.activation(gu_hi[:, u, :, :], raw_gu[:, :, u * P:(u + 1) * P], ACT.Copy).then_inc(s_guh, 1)

            def split_down(l, i, u):
                g, n = l * NG + i, l * NF + 2 * i + u
                act.wait_ge(s_rwd, 16 * n + 16)
                act.wait_ge(s_dmm, NCH * (g + 1))
                act.activation(wd_hi[:, u, :], raw_wd[:, :], ACT.Copy).then_inc(s_wdh, 1)

            def gated(l, i, u, par):
                for h in range(2):
                    n = 2 * (l * NF + 2 * i + u) + h
                    act.wait_ge(s_gumm, n + 1)
                    if not (isinstance(n, int) and n < 2):
                        act.wait_ge(s_a32, n - 1)
                    act.activation(sil[:, h, :], ps[h][:, :], ACT.Silu).then_inc(s_sil, 1)
                    act.wait_ge(s_a32, n + 1)
                    act.activation(a_hi[:, par, u, half(h)], a32[:, h, :], ACT.Copy).then_inc(s_ahi, 1)

            def body(l, i, par, last):
                if not last:
                    split_gate_up(l, i + 1, 0)
                split_down(l, i, 0)
                gated(l, i, 1, par)
                if not last:
                    split_gate_up(l, i + 1, 1)
                split_down(l, i, 1)
                if not last:
                    gated(l, i + 1, 0, 1 - par)

            def ffn(l):
                split_gate_up(l, 0, 0)
                split_gate_up(l, 0, 1)
                gated(l, 0, 0, 0)
                with act.Fori(0, NG // 2) as j:
                    body(l, 2 * j, 0, False)
                    body(l, 2 * j + 1, 1, False)
                body(l, NG - 1, 0, True)

            def x_complete(e, h):
                e.wait_ge(s_xadd, NCH * (NG + 1) - (KD if h == 0 else 0))

            def split_x(h):
                x_complete(act, h)
                for k in range(KD):
                    act.activation(hi_x[:, k, half(h)], xT[:, k, half(h)], ACT.Copy).then_inc(s_xch, 1)

            def latents():
                act.wait_ge(s_gumm, 2 * NF)
                split_x(0)
                for k in range(KD):
                    if k == 0:
                        act.wait_ge(s_dmm, NCH * (NG + 1))
                    act.wait_ge(s_cr[k % 4], 32 * (k // 4 + 1))
                    act.activation(wc_hi[:, k, 0:RL], raw_c[:, k % 4, 0:RL], ACT.Copy, scale=gain("ln_kv", k))
                    act.activation(wc_hi[:, k, RL:CW], raw_c[:, k % 4, RL:CW], ACT.Copy,
                                   scale=gain("ln_mix_b", k)).then_inc(s_wch, 1)
                squares(1, 0, x_complete)
                split_x(1)
                squares(1, 1, x_complete)
                for t in range(NT):
                    b = 4 * (t % 2)
                    act.wait_ge(s_cmm, t + 1)
                    act.wait_ge(s_r, 2 + t // 4 + 1)
                    r = rms[:, t:t + 1]
                    if t >= 1:
                        act.wait_ge(s_csq, t)
                    act.activation(junk[:, 0:KVR], ps[b][:, 0:KVR], ACT.Square, scale=r, accum_out=ssl[:, t, 0:1])
                    act.activation(junk[:, KVR:RL], ps[b + 1][:, 0:ROPE], ACT.Square, scale=r, accum_out=sskpe[:, t:t + 1])
                    act.activation(junk[:, RL:CW], ps[b + 1][:, ROPE:ROPE + QR], ACT.Square, scale=r,
                                   accum_out=ssl[:, t, 1:2]).then_inc(s_csq, 1)
                    if t >= 1:
                        latent_hi(t - 1)
                latent_hi(NT - 1)

            def latent_hi(t):
                act.wait_ge(s_ctr, t + 1)
                if t == 0:
                    act.wait_ge(s_spill, 32)
                    act.wait_ge(s_xcl, 2 * KD)
                tok = slice(t * P, (t + 1) * P)
                act.activation(cT_hi[:, :, tok], ps[6][:, :].rearrange("p (k t) -> p k t", t=P), ACT.Copy)
                act.activation(cqT_hi[:, :, tok], ps[7][:, 0:KQ * P].rearrange("p (k t) -> p k t", t=P),
                               ACT.Copy).then_inc(s_chi, 1)

            def split_unit(slot, nk, name, arrived, before):
                act.wait_ge(s_dwr[slot], arrived)
                if before is not None:
                    act.wait_ge(*before)
                for k in range(nk):
                    ins = act.activation(dw_hi[:, slot, k, :], dw_raw[:, slot, k, :], ACT.Copy, scale=gain(name, k))
                ins.then_inc(s_dwh, 1)

            def head_squares(b):
                p = b // 4
                src = (kn, qn)[p // 4][:, 2 * (p % 4) + (b // 2) % 2, half(b % 2)]
                act.wait_ge(s_kev, b + 1)
                if b == 0:
                    act.wait_ge(s_krtr, 2)
                if b >= 2:
                    act.wait_ge(s_kst, b - 1)
                act.activation(dsq[:, b % 2, :], src, ACT.Square).then_inc(s_ksq, 1)

            def heads():
                act.wait_ge(s_wcl, KD)
                split_unit(0, KC, "g_kv_latent", 16, None)
                split_unit(1, KC, "g_kv_latent", 16, None)
                with act.Fori(0, 2) as j:
                    for u in range(2):
                        split_unit(u, KC, "g_kv_latent", 16 * j + 32, (s_vmm, 16 * j + 8 * u + 8))
                for p in range(4):
                    for b in range(4 * p, 4 * p + 4):
                        head_squares(b)
                    if p < 2:
                        split_unit(p % 2, KC, "g_kv_latent", 64, (s_kmm, 4 * (p + 1)))
                    else:
                        split_unit(p % 2, KQ, "g_q_latent", 96, (s_kmm, 4 * (p + 1)))
                for n in range(8):
                    act.wait_ge(s_qrmm, n + 1)
                    if n >= 1:
                        act.wait_ge(s_qg, n)
                    act.activation(qsq[:, :, :, :], ps[n % 2][:, :].rearrange("p (t h c) -> p t h c", t=2, c=ROPE),
                                   ACT.Square).then_inc(s_qsq, 1)
                    if n % 4 == 3:
                        split_unit(n // 4, KQ, "g_q_latent", 128, (s_qrmm, n + 1))
                for p in range(4, 8):
                    for b in range(4 * p, 4 * p + 4):
                        head_squares(b)
                    if p < 6:
                        split_unit(p % 2, KQ, "g_q_latent", 160, (s_kmm, 4 * (p + 1)))

            def prepare_keys(h, u, f):
                act.wait_ge(s_kf, 2 * h + f + 1)
                act.activation(kr1[:, u, half(f)], krs[:, :], ACT.Copy)
                act.activation(khi[:, u, half(f)], kn[:, h, half(f)], ACT.Copy).then_inc(s_khi, 1)

            def prepare_queries(h, u):
                act.wait_ge(s_qpe, 8)
                act.activation(qhl[:, :, 0, :], qpe[:, :, h, :], ACT.Copy)
                act.activation(qhi[:, u, :], qn[:, h, :], ACT.Copy).then_inc(s_qh, 1)

            def query_part(h, u, f):
                act.wait_ge(s_qtr, 2 * h + f + 1)
                act.activation(qs[:, u, half(f)], ps[7][:, :], ACT.Copy).then_inc(s_qs, 1)

            def values(h):
                act.wait_ge(s_vev, 32)
                act.activation(v_hi[:, :, :], v32[:, :, bass.ds(h * P, P)], ACT.Copy).then_inc(s_vh, 1)

            def exponentials(h, m):
                n = h * NT + m
                w = (m + 1) * P
                act.wait_ge(s_nb, n + 1)
                if not (isinstance(n, int) and n < 2):
                    act.wait_ge(s_ptr, 12 * h + TR[m - 2] if m >= 2 else 12 * h - 12 + TR[m + 6])
                act.wait_ge(s_rqs, 1)
                act.activation(e32[:, m % 2, 0:w], ps_scores[m % 2][:, 0:w], ACT.Exp, scale=rq[:, h, m:m + 1],
                               bias=nb[:, m % 2:m % 2 + 1], accum_out=esum[:, m % 2:m % 2 + 1]).then_inc(s_exp, 1)

            def probabilities(h, m):
                n = h * NT + m
                w = (m + 1) * P
                act.wait_ge(s_rs, n + 1)
                act.activation(e32[:, m % 2, 0:w], e32[:, m % 2, 0:w], ACT.Copy,
                               scale=rsum[:, m % 2:m % 2 + 1]).then_inc(s_p, 1)

            def transposed_hi(h, m):
                if m % 2 == 0 and not (isinstance(h, int) and h == 0 and m == 0):
                    act.wait_ge(s_pv, 4 * h + m // 2)
                for c in range(m // 4 + 1):
                    nb_ = min(4, m + 1 - 4 * c)
                    g = 12 * h + TR[m] - m // 4 + c
                    act.wait_ge(s_ptr, g)
                    act.activation(pt_hi[:, 4 * c:4 * c + nb_, (m % 2) * P:(m % 2 + 1) * P],
                                   ps[4 + (TR[m] - m // 4 + c - 1) % 2][:, 0:nb_ * P].rearrange("p (k q) -> p k q", q=P),
                                   ACT.Copy).then_inc(s_pth, 1)

            def out_tile(h, j):
                act.activation(qn[:, h, 2 * P * j:2 * P * (j + 1)], ps[6][:, 0:2 * P], ACT.Copy).then_inc(s_o, 1)

            def head(h, u, first, last):
                for m in range(NT):
                    exponentials(h, m)
                    if not (first and m < 2):
                        transposed_hi(*((h, m - 2) if m >= 2 else (h - 1, m + 6)))
                        if m in (0, 2) and not first:
                            out_tile(h - 1, 2 + m // 2)
                        if m == 2 and not first:
                            values(h)
                        if m in (4, 6):
                            out_tile(h, m // 2 - 2)
                    probabilities(h, m)
                    if not last:
                        if m == 1:
                            prepare_queries(h + 1, 1 - u)
                        if m in (2, 4):
                            prepare_keys(h + 1, 1 - u, m // 2 - 1)
                        if m in (5, 6):
                            query_part(h + 1, 1 - u, m - 5)

            def attention():
                act.wait_ge(s_kst, 32)
                act.wait_ge(s_rqs, 1)
                prepare_queries(0, 0)
                for f in range(2):
                    prepare_keys(0, 0, f)
                for f in range(2):
                    query_part(0, 0, f)
                values(0)
                head(0, 0, True, False)
                with act.Fori(0, 3) as j:
                    for w in range(2):
                        head(2 * j + 1 + w, 1 - w, False, False)
                head(NH - 1, 1, False, True)
                transposed_hi(NH - 1, 6)
                out_tile(NH - 1, 2)
                transposed_hi(NH - 1, 7)
                act.wait_ge(s_pv, 4 * NH)
                out_tile(NH - 1, 3)

            def output_projection():
                act.wait_ge(s_o, 4 * NH)
                for k in range(NH):
                    act.activation(hi_x[:, k, :], qn[:, k, :], ACT.Copy).then_inc(s_oh, 1)
                    if k == 0:
                        split_wo(0)
                split_wo(1)
                split_wo(2)
                split_wo(3)

            def split_wo(u):
                act.wait_ge(s_wor[u % 2], 16 * (u // 2 + 1))
                if u >= 2:
                    act.wait_ge(s_omm, 4 * (u - 1))
                act.activation(wo_hi[:, u % 2, :, :], wo_raw[:, u % 2, :, :], ACT.Copy).then_inc(s_woh, 1)

            norm(0, 0, lambda e, h: e.wait_ge(s_xadd, 16))
            ffn(0)
            if stage == 2:
                norm(1, 1, lambda e, h: e.wait_ge(s_xadd, NCH * (NG + 1) - (KD if h == 0 else 0)))
                ffn(1)
            if stage >= 3:
                latents()
                heads()
                attention()
                output_projection()
                norm(2, 1, lambda e, h: e.wait_ge(s_ox, NCH))
                ffn(1)
            for t in range(NT):
                act.wait_ge(s_otr, 2 * t + 2)
                act.activation(xtok[:, t, 512:1024], ps[5 + 2 * (t % 2)][:, :], ACT.Copy).then_inc(s_oev2, 1)

        @block.vector
        def _(dve):
            steps = [0]

            def link(ins):
                steps[0] += 1
                ins.then_inc(s_dve, 1)
                dve.wait_ge(s_dve, steps[0])

            ang, whole, big, cut, sin_in, cos_in = (tab[:, i, :, :] for i in range(6))
            dve.wait_ge(s_pos, 16)
            dve.wait_ge(s_const, NCONST)
            dve.tensor_copy(pos_row[:, :], pos_i[:, :]).then_inc(s_posf, 1)
            dve.wait_ge(s_posT, 1)
            link(dve.tensor_copy(pos_f[:, :], ps[3][:, 0:NT]))
            link(dve.tensor_tensor(ang, pos_f[:, :].unsqueeze(2).broadcast_to([P, NT, HR]),
                                   inv_t[:, :].unsqueeze(1).broadcast_to([P, NT, HR]), ALU.mult))
            link(dve.tensor_scalar(whole, ang, 1.0 / TWO_PI, MAGIC, ALU.mult, ALU.add))
            link(dve.tensor_scalar(whole, whole, MAGIC, None, ALU.subtract))
            link(dve.tensor_scalar(big, whole, MAGIC * 2048, None, ALU.add))
            link(dve.tensor_scalar(big, big, MAGIC * 2048, None, ALU.subtract))
            link(dve.tensor_tensor(whole, whole, big, ALU.subtract))
            for c in pieces(TWO_PI, 4):
                for turns in (big, whole):
                    link(dve.scalar_tensor_tensor(out=ang, in0=turns, scalar=-c, in1=ang, op0=ALU.mult, op1=ALU.add))
            link(dve.tensor_scalar(sin_in, ang, 3.1415925, -3.1415925, ALU.min, ALU.max))
            dve.scalar_tensor_tensor(out=cos_in, in0=sin_in, scalar=-1.0, in1=sin_in, op0=ALU.mult,
                                     op1=ALU.max).then_inc(s_ang, 1)
            dve.wait_ge(s_gT, 1)
            dve.tensor_copy(gT[:, :], ps[2][:, 0:NROW]).then_inc(s_gc, 1)
            dve.wait_ge(s_gc, 1)
            dve.tensor_tensor(bs[:, :], gT[:, ROW["b_pool"]:ROW["b_pool"] + 8],
                              gT[:, ROW["pool_scale"]:ROW["pool_scale"] + 8], ALU.mult).then_inc(s_bs, 1)
            for t in range(NT):
                for b in range(2):
                    dve.wait_ge(s_xtr, 2 * t + b + 1)
                    dve.tensor_copy(xT[:, 4 * b:4 * b + 4, t * P:(t + 1) * P],
                                    ps[4 + 2 * (t % 2) + b][:, :].rearrange("p (k t) -> p k t", t=P)).then_inc(s_xev, 1)
                dve.wait_ge(s_rA, t + 1)
                dve.tensor_scalar(diagA[:, t, :], ident[:, :], rms[:, t:t + 1], None, ALU.mult).then_inc(s_dgA, 1)
            dve.wait_ge(s_wph, 1)
            dve.tensor_tensor(wp_lo[:, :, :], wp_raw[:, :, :], wp_hi[:, :, :].bitcast(F), ALU.subtract).then_inc(s_wpl, 1)
            dve.wait_ge(s_bcA, NT)
            dve.wait_ge(s_xev, 2 * NT)

            def make_h(g):
                for kk in range(2):
                    k = 2 * g + kk
                    for h in range(2):
                        if g >= 2:
                            dve.wait_ge(s_dlo, g - 1)
                        ins = dve.scalar_tensor_tensor(out=hp[:, g % 2, kk, half(h)], in0=xT[:, k, half(h)],
                                                       scalar=gain("ln_mix_a", k), in1=ps[h][:, :],
                                                       op0=ALU.mult, op1=ALU.mult)
                ins.then_inc(s_h, 1)

            win_steps = 0

            def make_d(g):
                w = WINDOWS[g]
                s = (sA, sB)[g % 2]
                dve.wait_ge(s_win, 2 * sum(range(1, g + 2)))
                dve.wait_ge(s_h, g + 1)
                link(dve.tensor_tensor(edge[:, :, 0:w], s[:, :, 0:w],
                                       invc[:, 0:w].unsqueeze(1).broadcast_to([P, 2, w]), ALU.mult))
                link(dve.tensor_tensor(edge[:, :, 0:w], edge[:, :, 0:w], hp[:, g % 2, :, 0:w], ALU.subtract))
                link(dve.scalar_tensor_tensor(out=hp[:, g % 2, :, :], in0=s[:, :, :], scalar=1.0 / w,
                                              in1=hp[:, g % 2, :, :], op0=ALU.mult, op1=ALU.subtract))
                dve.tensor_copy(hp[:, g % 2, :, 0:w], edge[:, :, 0:w]).then_inc(s_d32, 1)

            def split_d(g):
                dve.wait_ge(s_dhi, g + 1)
                dve.tensor_tensor(lo_x[:, 2 * g:2 * g + 2, :], hp[:, g % 2, :, :],
                                  hi_x[:, 2 * g:2 * g + 2, :].bitcast(F), ALU.subtract).then_inc(s_dlo, 1)

            def add_y(n):
                g, dt, h = n // 4, (n // 2) % 2, n % 2
                x = xT[:, 2 * g + dt, half(h)]
                dve.wait_ge(s_py, n + 1)
                dve.tensor_tensor(x, x, ytmp[:, n % 2, :], ALU.add).then_inc(s_xadd, 1)

            make_h(0)
            make_h(1)
            for g in range(4):
                make_d(g)
                split_d(g)
                if g + 2 < 4:
                    make_h(g + 2)
                if g >= 1:
                    for n in range(4 * g - 4, 4 * g):
                        add_y(n)
            for n in range(12, 16):
                add_y(n)

            def square_sums(q, h):
                dve.wait_ge(s_ssm, (2 * q + h + 1) * KD)
                dve.tensor_copy(ss[:, 4 * h:4 * h + 4], ps[2 + h][:, 0:4]).then_inc(s_ss, 1)

            def norm(q, l, name):
                square_sums(q, 0)
                square_sums(q, 1)
                for h in range(2):
                    dve.wait_ge(s_r, 2 * q + h + 1)
                    if h == 1:
                        dve.wait_ge(s_bc, 2 * l + 1)
                    for t in range(4):
                        ins = dve.tensor_scalar(diag[:, t, :], ident[:, :], rms[:, 4 * h + t:4 * h + t + 1], None, ALU.mult)
                    ins.then_inc(s_dg, 1)
                for h in range(2):
                    dve.wait_ge(s_bc, 2 * l + h + 1)
                    for k in range(KD):
                        n = (2 * l + h) * KD + k
                        if n >= 2:
                            dve.wait_ge(s_hlo, n - 1)
                        dve.scalar_tensor_tensor(out=sq[:, k % 2, :], in0=xT[:, k, half(h)], scalar=gain(name, k),
                                                 in1=ps[h][:, :], op0=ALU.mult, op1=ALU.mult).then_inc(s_h32, 1)
                        if k >= 1:
                            low(n - 1, h, k - 1)
                    low((2 * l + h) * KD + KD - 1, h, KD - 1)

            def low(n, h, k):
                dve.wait_ge(s_hhi, n + 1)
                dve.tensor_tensor(lo_x[:, k, half(h)], sq[:, k % 2, :], hi_x[:, k, half(h)].bitcast(F),
                                  ALU.subtract).then_inc(s_hlo, 1)

            def split_gate_up(l, i, u):
                n = l * NF + 2 * i + u
                dve.wait_ge(s_guh, n + 1)
                dve.tensor_tensor(gu_lo[:, u, :, :], raw_gu[:, :, u * P:(u + 1) * P], gu_hi[:, u, :, :].bitcast(F),
                                  ALU.subtract).then_inc(s_gul, 1)

            def split_down(l, i, u):
                n = l * NF + 2 * i + u
                dve.wait_ge(s_wdh, n + 1)
                dve.tensor_tensor(wd_lo[:, u, :], raw_wd[:, :], wd_hi[:, u, :].bitcast(F),
                                  ALU.subtract).then_inc(s_wdl, 1)

            def gated(l, i, u, par):
                for h in range(2):
                    n = 2 * (l * NF + 2 * i + u) + h
                    dve.wait_ge(s_sil, n + 1)
                    dve.tensor_tensor(a32[:, h, :], sil[:, h, :], ps[2 + h][:, :], ALU.mult).then_inc(s_a32, 1)
                    dve.wait_ge(s_ahi, n + 1)
                    dve.tensor_tensor(a_lo[:, par, u, half(h)], a32[:, h, :], a_hi[:, par, u, half(h)].bitcast(F),
                                      ALU.subtract).then_inc(s_alo, 1)

            def add_down(l, i):
                g = l * NG + i
                dve.wait_ge(s_xadd, NCH * (g + 1))
                for c in range(NCH):
                    h, k = c // KD, c % KD
                    x = xT[:, k, half(h)]
                    dve.wait_ge(s_dmm, NCH * (g + 1) + c + 1)
                    dve.tensor_tensor(x, x, ps[4 + c % 4][:, :], ALU.add).then_inc(s_xadd, 1)

            def body(l, i, par, last):
                if not last:
                    split_gate_up(l, i + 1, 0)
                split_down(l, i, 0)
                gated(l, i, 1, par)
                if not last:
                    split_gate_up(l, i + 1, 1)
                split_down(l, i, 1)
                if not last:
                    gated(l, i + 1, 0, 1 - par)
                add_down(l, i)

            def ffn(l):
                split_gate_up(l, 0, 0)
                split_gate_up(l, 0, 1)
                gated(l, 0, 0, 0)
                with dve.Fori(0, NG // 2) as j:
                    body(l, 2 * j, 0, False)
                    body(l, 2 * j + 1, 1, False)
                body(l, NG - 1, 0, True)

            def latents():
                for k in range(KD):
                    dve.wait_ge(s_wch, k + 1)
                    for cols, name in ((slice(0, RL), "ln_kv"), (slice(RL, CW), "ln_mix_b")):
                        ins = dve.scalar_tensor_tensor(out=wc_lo[:, k, cols], in0=raw_c[:, k % 4, cols], scalar=gain(name, k),
                                                       in1=wc_hi[:, k, cols].bitcast(F), op0=ALU.mult, op1=ALU.subtract)
                    ins.then_inc(s_wcl, 1)
                square_sums(1, 0)
                square_sums(1, 1)
                for t in range(NT):
                    b = 4 * (t % 2)
                    dve.wait_ge(s_rl, t + 1)
                    if t >= 2:
                        dve.wait_ge(s_ctr, t - 1)
                    r = rms[:, t:t + 1]
                    dve.tensor_scalar(kpe[:, t, :], ps[b + 1][:, 0:ROPE], r, None, ALU.mult)
                    dve.tensor_scalar(c_tok[:, t % 2, 0:KVR], ps[b][:, 0:KVR], r, rl[:, t, 0:1], ALU.mult, ALU.mult)
                    dve.tensor_scalar(c_tok[:, t % 2, KVR:KVR + QR], ps[b + 1][:, ROPE:ROPE + QR], r, rl[:, t, 1:2],
                                      ALU.mult, ALU.mult).then_inc(s_ctok, 1)
                    if t >= 1:
                        latent_lo(t - 1)
                latent_lo(NT - 1)

            def latent_lo(t):
                dve.wait_ge(s_chi, t + 1)
                tok = slice(t * P, (t + 1) * P)
                dve.tensor_tensor(cT_lo[:, :, tok], ps[6][:, :].rearrange("p (k t) -> p k t", t=P),
                                  cT_hi[:, :, tok].bitcast(F), ALU.subtract)
                dve.tensor_tensor(cqT_lo[:, :, tok], ps[7][:, 0:KQ * P].rearrange("p (k t) -> p k t", t=P),
                                  cqT_hi[:, :, tok].bitcast(F), ALU.subtract).then_inc(s_clo, 1)

            def split_unit(slot, nk, name, u):
                dve.wait_ge(s_dwh, u + 1)
                for k in range(nk):
                    ins = dve.scalar_tensor_tensor(out=dw_lo[:, slot, k, :], in0=dw_raw[:, slot, k, :], scalar=gain(name, k),
                                                   in1=dw_hi[:, slot, k, :].bitcast(F), op0=ALU.mult, op1=ALU.subtract)
                ins.then_inc(s_dwl, 1)

            def rotate_key_part():
                dve.wait_ge(s_gr, 32)
                dve.wait_ge(s_tab, 1)
                link(dve.tensor_tensor(kg[:, :, :], kpe[:, :, :],
                                       g_rope[:, 0, :].unsqueeze(1).broadcast_to([P, NT, ROPE]), ALU.mult))
                x1, x2 = kg[:, :, 0:HR], kg[:, :, HR:ROPE]
                for part, (p, q, op) in enumerate(((x1, x2, ALU.subtract), (x2, x1, ALU.add))):
                    dve.tensor_tensor(krt[:, 0, :, :], p, cos_t[:, :, :], ALU.mult)
                    link(dve.tensor_tensor(krt[:, 1, :, :], q, sin_t[:, :, :], ALU.mult))
                    for twice in range(2):
                        ins = dve.tensor_tensor(krd[:, :, twice, part * HR:(part + 1) * HR], krt[:, 0, :, :],
                                                krt[:, 1, :, :], op)
                    if part == 0:
                        link(ins)
                ins.then_inc(s_krd, 1)

            def evacuate_heads(b):
                p = b // 4
                dve.wait_ge(s_kmm, b + 1)
                dve.tensor_copy((kn, qn)[p // 4][:, 2 * (p % 4) + (b // 2) % 2, half(b % 2)],
                                ps[4 + b % 2][:, :]).then_inc(s_kev, 1)

            def head_sums(p):
                pair = slice(2 * (p % 4), 2 * (p % 4) + 2)
                rotated = sskpe[:, :].unsqueeze(1).broadcast_to([P, 2, NT]) if p < 4 else ssqpe[:, pair, :]
                dve.wait_ge(s_kst, 4 * p + 4)
                dve.tensor_tensor((rk, rq)[p // 4][:, pair, :], ps[3 + 4 * (1 - p % 2)][:, 0:16].rearrange("p (h t) -> p h t", t=NT),
                                  rotated, ALU.add).then_inc(s_kstc, 1)

            def rotate_queries(n):
                u, c = n // 4, n % 4
                tok, hd = slice(2 * c, 2 * c + 2), slice(4 * u, 4 * u + 4)
                dve.wait_ge(s_qsq, n + 1)
                dve.reduce_sum(ssqpe[:, hd, tok].rearrange("p h t -> p t h"), qsq[:, :, :, :], axis=AX.X)
                if n >= 1:
                    dve.wait_ge(s_qcs, n)
                for i in range(2):
                    ins = dve.tensor_tensor(qg[:, i, :, :], ps[n % 2][:, 256 * i:256 * i + 256].rearrange("p (h c) -> p h c", c=ROPE),
                                            g_rope[:, 1, :].unsqueeze(1).broadcast_to([P, 4, ROPE]), ALU.mult)
                ins.then_inc(s_qg, 1)
                dve.wait_ge(s_qg, n + 1)
                if n >= 1:
                    dve.wait_ge(s_qpe, n)
                dve.tensor_tensor(rt[:, 0, :, :, :], qg[:, :, :, 0:HR], table(cos_t, c), ALU.mult)
                link(dve.tensor_tensor(rt[:, 1, :, :, :], qg[:, :, :, HR:ROPE], table(sin_t, c), ALU.mult))
                dve.tensor_tensor(qpe[:, tok, hd, 0:HR], rt[:, 0, :, :, :], rt[:, 1, :, :, :], ALU.subtract)
                dve.wait_ge(s_qcs, n + 1)
                dve.tensor_tensor(qpe[:, tok, hd, HR:ROPE], rt[:, 2, :, :, :], rt[:, 3, :, :, :], ALU.add).then_inc(s_qpe, 1)

            def heads():
                split_unit(0, KC, "g_kv_latent", 0)
                split_unit(1, KC, "g_kv_latent", 1)
                rotate_key_part()
                dve.tensor_tensor(gkq[:, :], gain("g_k", 0), gain("g_q", 0), ALU.mult)
                with dve.Fori(0, 2) as j:
                    for u in range(2):
                        n = 2 * j + u
                        for t in range(NT):
                            dve.wait_ge(s_vmm, 8 * n + t + 1)
                            dve.tensor_copy(v32[:, t, bass.ds(n * 2 * P, 2 * P)], ps[t % 4][:, 0:2 * P]).then_inc(s_vev, 1)
                        split_unit(u, KC, "g_kv_latent", n + 2)
                for f in range(2):
                    dve.wait_ge(s_krtr, f + 1)
                    dve.tensor_copy(krT[:, half(f)], ps[4 + f][:, :]).then_inc(s_krT, 1)
                for p in range(8):
                    for b in range(4 * p, 4 * p + 4):
                        evacuate_heads(b)
                        if b % 4 == 0 and p % 4 > 0:
                            head_sums(p - 1)
                    if p < 4:
                        split_unit(p % 2, KC if p < 2 else KQ, "g_kv_latent" if p < 2 else "g_q_latent", 6 + p)
                    elif p < 6:
                        split_unit(p % 2, KQ, "g_q_latent", 8 + p)
                    if p % 4 == 3:
                        head_sums(p)
                    if p == 3:
                        for n in range(8):
                            rotate_queries(n)
                            if n % 4 == 3:
                                split_unit(n // 4, KQ, "g_q_latent", 10 + n // 4)
                dve.wait_ge(s_rk, 8)
                link(dve.tensor_scalar(rq[:, :, :], rq[:, :, :], SCALE, None, ALU.mult))
                dve.tensor_scalar(nrq[:, :, :], rq[:, :, :], -1.0, None, ALU.mult).then_inc(s_rqs, 1)
                dve.wait_ge(s_rqs, 1)

            def key_diag(h, f):
                if not (isinstance(h, int) and h == 0 and f == 0):
                    dve.wait_ge(s_kbc, 2 * h + f)
                for t in range(4):
                    ins = dve.tensor_scalar(kdiag[:, t, :], ident[:, :], rk[:, h, 4 * f + t:4 * f + t + 1], None, ALU.mult)
                ins.then_inc(s_kd, 1)

            def scale_keys(h, f):
                dve.wait_ge(s_kbc, 2 * h + f + 1)
                if not (isinstance(h, int) and h == 0 and f == 0):
                    dve.wait_ge(s_klo, 2 * h + f)
                dve.tensor_tensor(krs[:, :], krT[:, half(f)], ps[7][:, :], ALU.mult)
                dve.scalar_tensor_tensor(out=kn[:, h, half(f)], in0=kn[:, h, half(f)], scalar=gkq[:, 0:1],
                                         in1=ps[7][:, :], op0=ALU.mult, op1=ALU.mult).then_inc(s_kf, 1)

            def softmax_front(h, m):
                n, w, sc, i = h * NT + m, (m + 1) * P, ps_scores[m % 2], m % 2
                dve.wait_ge(s_sc, n + 1)
                dve.memset(sc[0:CHUNK, w - CHUNK:w], NEG).then_inc(s_mask, 1)
                dve.wait_ge(s_mask, n + 1)
                dve.reduce_max(mx[:, i:i + 1], sc[:, 0:w], axis=AX.X).then_inc(s_max, 1)
                dve.wait_ge(s_max, n + 1)
                dve.tensor_tensor(nb[:, i:i + 1], mx[:, i:i + 1], nrq[:, h, m:m + 1], ALU.mult).then_inc(s_nb, 1)

            def softmax_sums(h, m):
                n, i = h * NT + m, m % 2
                dve.wait_ge(s_exp, n + 1)
                if not (isinstance(n, int) and n < 2):
                    dve.wait_ge(s_p, n - 1)
                dve.reciprocal(rsum[:, i:i + 1], esum[:, i:i + 1]).then_inc(s_rs, 1)

            def transposed_lo(h, m):
                for c in range(m // 4 + 1):
                    nb_ = min(4, m + 1 - 4 * c)
                    part = (slice(None), slice(4 * c, 4 * c + nb_), slice((m % 2) * P, (m % 2 + 1) * P))
                    dve.wait_ge(s_pth, 12 * h + TR[m] - m // 4 + c)
                    dve.tensor_tensor(pt_lo[part],
                                      ps[4 + (TR[m] - m // 4 + c - 1) % 2][:, 0:nb_ * P].rearrange("p (k q) -> p k q", q=P),
                                      pt_hi[part].bitcast(F), ALU.subtract).then_inc(s_ptl, 1)

            def head(h, first, last):
                for m in range(NT):
                    softmax_front(h, m)
                    if not (first and m < 2):
                        transposed_lo(*((h, m - 2) if m >= 2 else (h - 1, m + 6)))
                    softmax_sums(h, m)
                    if not last:
                        if m == 0:
                            key_diag(h + 1, 0)
                        if m == 2:
                            scale_keys(h + 1, 0)
                            key_diag(h + 1, 1)
                        if m == 4:
                            scale_keys(h + 1, 1)

            def attention():
                for f in range(2):
                    key_diag(0, f)
                    scale_keys(0, f)
                head(0, True, False)
                with dve.Fori(0, 3) as j:
                    for w in range(2):
                        head(2 * j + 1 + w, False, False)
                head(NH - 1, False, True)
                transposed_lo(NH - 1, 6)
                transposed_lo(NH - 1, 7)

            def split_wo(u):
                dve.wait_ge(s_woh, u + 1)
                dve.tensor_tensor(wo_lo[:, u % 2, :, :], wo_raw[:, u % 2, :, :], wo_hi[:, u % 2, :, :].bitcast(F),
                                  ALU.subtract).then_inc(s_wol, 1)

            def output_projection():
                for k in range(NH):
                    dve.wait_ge(s_oh, k + 1)
                    dve.tensor_tensor(lo_x[:, k, :], qn[:, k, :], hi_x[:, k, :].bitcast(F), ALU.subtract).then_inc(s_ol, 1)
                    if k == 0:
                        split_wo(0)
                split_wo(1)
                dve.wait_ge(s_back, 32)
                for c in range(NCH):
                    x = xT[:, c // 2, half(c % 2)]
                    dve.wait_ge(s_omm, c + 1)
                    dve.tensor_tensor(x, x, ps[4 + c % 4][:, :], ALU.add).then_inc(s_ox, 1)
                    if c in (3, 7):
                        split_wo(c // 4 + 2)

            norm(0, 0, "ln_ffn0")
            ffn(0)
            if stage == 2:
                norm(1, 1, "ln_ffn1")
                ffn(1)
            if stage >= 3:
                latents()
                heads()
                attention()
                output_projection()
                norm(2, 1, "ln_ffn1")
                ffn(1)
            for t in range(NT):
                dve.wait_ge(s_otr, 2 * t + 1)
                dve.tensor_copy(xtok[:, t, 0:512], ps[4 + 2 * (t % 2)][:, :]).then_inc(s_oev, 1)

        @block.tensor
        def _(pe):
            def three(bank, terms, last_signal=None):
                n, m = 0, 3 * len(terms)
                for wh, wl, xh, xl in terms:
                    for w, x in ((wh, xh), (wh, xl), (wl, xh)):
                        ins = pe.matmul(bank, w, x, start=n == 0, stop=n == m - 1)
                        n += 1
                return ins

            pe.wait_ge(s_const, NCONST)
            pe.wait_ge(s_g, 16 * len(g_src))
            pe.wait_ge(s_posf, 1)
            pe.transpose(ps[3][:, 0:NT], pos_row[:, :], ident[0:NT, 0:NT]).then_inc(s_posT, 1)
            pe.transpose(ps[2][:, 0:NROW], grow[:, :], ident[0:NROW, 0:NROW]).then_inc(s_gT, 1)
            for t in range(NT):
                pe.wait_ge(s_x[t], 16)
                for b in range(2):
                    if t >= 2:
                        pe.wait_ge(s_xev, 2 * (t - 2) + b + 1)
                    for k in range(4):
                        ins = pe.transpose(ps[4 + 2 * (t % 2) + b][:, k * P:(k + 1) * P],
                                           xtok[:, t, (4 * b + k) * P:(4 * b + k + 1) * P], ident[:, :])
                    ins.then_inc(s_xtr, 1)
                if t >= 1:
                    pe.wait_ge(s_dgA, t)
                    pe.matmul(ps[(t - 1) // 4][:, (t - 1) % 4 * P:((t - 1) % 4 + 1) * P], ones[:, :],
                              diagA[:, t - 1, :], start=True, stop=True).then_inc(s_bcA, 1)
            pe.wait_ge(s_dgA, NT)
            pe.matmul(ps[1][:, 3 * P:4 * P], ones[:, :], diagA[:, NT - 1, :], start=True, stop=True).then_inc(s_bcA, 1)
            pe.wait_ge(s_xev, 2 * NT)
            pe.wait_ge(s_wpl, 1)
            for n in range(16):
                g, dt, h = n // 4, (n // 2) % 2, n % 2
                if n % 4 == 0:
                    pe.wait_ge(s_dlo, g + 1)
                if n >= 4:
                    pe.wait_ge(s_py, n - 3)
                three(ps[4 + n % 4][:, :], [(wp_hi[:, 2 * g + c, dt * P:(dt + 1) * P], wp_lo[:, 2 * g + c, dt * P:(dt + 1) * P],
                                             hi_x[:, 2 * g + c, half(h)], lo_x[:, 2 * g + c, half(h)])
                                            for c in range(2)]).then_inc(s_dmm, 1)

            def square_sums(q, h):
                for k in range(KD):
                    pe.wait_ge(s_sq, (2 * q + h) * KD + k + 1)
                    for t in range(4):
                        ins = pe.matmul(ps[2 + h][:, t:t + 1], sq[:, k % 2, t * P:(t + 1) * P], ones[:, 0:1],
                                        start=k == 0 and t == 0, stop=k == KD - 1, skip_group_check=True)
                    ins.then_inc(s_ssm, 1)

            def norm(q, l):
                square_sums(q, 0)
                square_sums(q, 1)
                for h in range(2):
                    pe.wait_ge(s_dg, 2 * l + h + 1)
                    for t in range(4):
                        ins = pe.matmul(ps[h][:, t * P:(t + 1) * P], ones[:, :], diag[:, t, :], start=True, stop=True)
                    ins.then_inc(s_bc, 1)

            def gate_up(l, i, u):
                n = l * NF + 2 * i + u
                pe.wait_ge(s_gul, n + 1)
                for h in range(2):
                    if not (isinstance(n, int) and n == 0):
                        pe.wait_ge(s_a32, 2 * n - 1 + h)
                    three(ps[h][:, :], [(gu_hi[:, u, k, :], gu_lo[:, u, k, :], hi_x[:, k, half(h)], lo_x[:, k, half(h)])
                                        for k in range(KD)])
                    three(ps[2 + h][:, :], [(gu_hi[:, u, KD + k, :], gu_lo[:, u, KD + k, :], hi_x[:, k, half(h)],
                                             lo_x[:, k, half(h)]) for k in range(KD)]).then_inc(s_gumm, 1)

            def down(l, i, par):
                g = l * NG + i
                pe.wait_ge(s_wdl, 2 * g + 2)
                pe.wait_ge(s_alo, 4 * g + 4)
                for c in range(NCH):
                    h, k = c // KD, c % KD
                    pe.wait_ge(s_xadd, NCH * (g + 1) + c - 3)
                    three(ps[4 + c % 4][:, :], [(wd_hi[:, u, k * P:(k + 1) * P], wd_lo[:, u, k * P:(k + 1) * P],
                                                 a_hi[:, par, u, half(h)], a_lo[:, par, u, half(h)])
                                                for u in range(2)]).then_inc(s_dmm, 1)

            def ffn(l):
                pe.wait_ge(s_hlo, 2 * KD * (l + 1))
                gate_up(l, 0, 0)
                with pe.Fori(0, NG // 2) as j:
                    for par in range(2):
                        i = 2 * j + par
                        gate_up(l, i, 1)
                        gate_up(l, i + 1, 0)
                        down(l, i, par)
                gate_up(l, NG - 1, 1)
                down(l, NG - 1, 0)

            def latents():
                square_sums(1, 0)
                square_sums(1, 1)
                pe.wait_ge(s_xcl, KD)
                for t in range(NT):
                    b, tok = 4 * (t % 2), slice(t * P, (t + 1) * P)
                    if t == 4:
                        pe.wait_ge(s_xcl, 2 * KD)
                    if t >= 2:
                        pe.wait_ge(s_ctok, t - 1)
                    for k in range(KD):
                        if t == 0:
                            pe.wait_ge(s_wcl, k + 1)
                        n = 0
                        for x, w in ((hi_x, wc_hi), (hi_x, wc_lo), (lo_x, wc_hi)):
                            first, last = k == 0 and n == 0, k == KD - 1 and n == 2
                            pe.matmul(ps[b][:, 0:KVR], x[:, k, tok], w[:, k, 0:KVR], start=first, stop=last)
                            ins = pe.matmul(ps[b + 1][:, 0:ROPE + QR], x[:, k, tok], w[:, k, KVR:CW], start=first, stop=last)
                            n += 1
                    ins.then_inc(s_cmm, 1)
                    if t >= 1:
                        transpose_latents(t - 1)
                transpose_latents(NT - 1)

            def transpose_latents(t):
                pe.wait_ge(s_ctok, t + 1)
                if t >= 1:
                    pe.wait_ge(s_clo, t)
                for k in range(KC):
                    pe.transpose(ps[6][:, k * P:(k + 1) * P], c_tok[:, t % 2, k * P:(k + 1) * P], ident[:, :])
                for k in range(KQ):
                    ins = pe.transpose(ps[7][:, k * P:(k + 1) * P], c_tok[:, t % 2, KVR + k * P:KVR + (k + 1) * P], ident[:, :])
                ins.then_inc(s_ctr, 1)

            def head_product(b):
                p, hh, f = b // 4, (b // 2) % 2, b % 2
                nk, x_hi, x_lo = (KC, cT_hi, cT_lo) if p < 4 else (KQ, cqT_hi, cqT_lo)
                if b % 4 == 0:
                    pe.wait_ge(s_dwl, p + 5 if p < 4 else p + 7)
                if b >= 2:
                    pe.wait_ge(s_kev, b - 1)
                cols = slice(hh * P, (hh + 1) * P)
                three(ps[4 + b % 2][:, :], [(dw_hi[:, p % 2, k, cols], dw_lo[:, p % 2, k, cols], x_hi[:, k, half(f)],
                                             x_lo[:, k, half(f)]) for k in range(nk)]).then_inc(s_kmm, 1)

            def head_square_sums(b):
                p = b // 4
                pe.wait_ge(s_ksq, b + 1)
                if b % 4 == 0 and p >= 2:
                    pe.wait_ge(s_kstc, p - 1)
                bank = ps[3 + 4 * (1 - p % 2)]
                for t in range(4):
                    col = 4 * (b % 4) + t
                    ins = pe.matmul(bank[:, col:col + 1], dsq[:, b % 2, t * P:(t + 1) * P], ones[:, 0:1], start=True, stop=True)
                ins.then_inc(s_kst, 1)

            def heads():
                pe.wait_ge(s_clo, NT)
                for n in range(4):
                    pe.wait_ge(s_dwl, n + 1)
                    for t in range(NT):
                        tok = slice(t * P, (t + 1) * P)
                        if 8 * n + t >= 4:
                            pe.wait_ge(s_vev, 8 * n + t - 3)
                        three(ps[t % 4][:, 0:2 * P], [(cT_hi[:, k, tok], cT_lo[:, k, tok], dw_hi[:, n % 2, k, :],
                                                       dw_lo[:, n % 2, k, :]) for k in range(KC)]).then_inc(s_vmm, 1)
                pe.wait_ge(s_krd, 1)
                for f in range(2):
                    for t in range(4):
                        ins = pe.transpose(ps[4 + f][:, t * P:(t + 1) * P],
                                           krd[:, 4 * f + t, :, :].rearrange("p a c -> p (a c)"), ident[:, :])
                    ins.then_inc(s_krtr, 1)
                pe.wait_ge(s_krT, 2)
                pe.wait_ge(s_vev, 32)
                for b in range(32):
                    if b == 16:
                        head_square_sums(15)
                        for n in range(8):
                            u, c = n // 4, n % 4
                            if c == 0:
                                pe.wait_ge(s_dwl, 9 + u)
                            if n >= 2:
                                pe.wait_ge(s_qg, n - 1)
                            for i in range(2):
                                tok = slice((2 * c + i) * P, (2 * c + i + 1) * P)
                                ins = three(ps[n % 2][:, 2 * P * i:2 * P * (i + 1)],
                                            [(cqT_hi[:, k, tok], cqT_lo[:, k, tok], dw_hi[:, u, k, :], dw_lo[:, u, k, :])
                                             for k in range(KQ)])
                            ins.then_inc(s_qrmm, 1)
                    head_product(b)
                    if b % 16 > 0:
                        head_square_sums(b - 1)
                head_square_sums(31)

            def key_rms(h, f):
                pe.wait_ge(s_kd, 2 * h + f + 1)
                if f == 1:
                    pe.wait_ge(s_kf, 2 * h + 1)
                elif not (isinstance(h, int) and h == 0):
                    pe.wait_ge(s_qs, 2 * h)
                for t in range(4):
                    ins = pe.matmul(ps[7][:, t * P:(t + 1) * P], ones[:, :], kdiag[:, t, :], start=True, stop=True)
                ins.then_inc(s_kbc, 1)

            def query_part(h, f):
                pe.wait_ge(s_qhl, h + 1)
                pe.wait_ge(s_kf, 2 * h + 2)
                if f == 1:
                    pe.wait_ge(s_qs, 2 * h + 1)
                for t in range(4):
                    ins = pe.transpose(ps[7][:, t * P:(t + 1) * P],
                                       qhl[:, 4 * f + t, :, :].rearrange("p a c -> p (a c)").bitcast(F), ident[:, :])
                ins.then_inc(s_qtr, 1)

            def scores(h, u, m):
                n, w, q = h * NT + m, (m + 1) * P, slice(m * P, (m + 1) * P)
                if m == 0:
                    pe.wait_ge(s_klo, 2 * h + 2)
                    pe.wait_ge(s_ql, h + 1)
                    pe.wait_ge(s_qs, 2 * h + 2)
                if not (isinstance(n, int) and n < 2):
                    pe.wait_ge(s_exp, n - 1)
                for c in range(m // 4 + 1):
                    keys = slice(c * 512, min(w, (c + 1) * 512))
                    terms = ((qhi, khi[:, u, keys]), (qhi, klo[:, h, keys]), (qlo, khi[:, u, keys]),
                             (qs, kr1[:, u, keys]), (qs, kr2[:, u, keys]))
                    for i, (query, key) in enumerate(terms):
                        ins = pe.matmul(ps_scores[m % 2][:, keys], query[:, u, q], key, start=i == 0, stop=i == 4)
                ins.then_inc(s_sc, 1)

            def transposes(h, m):
                pe.wait_ge(s_p, h * NT + m + 1)
                for c in range(m // 4 + 1):
                    g = TR[m] - m // 4 + c
                    if not (isinstance(h, int) and h == 0 and g <= 2):
                        pe.wait_ge(s_ptl, 12 * h + g - 2)
                    for k in range(min(4, m + 1 - 4 * c)):
                        ins = pe.transpose(ps[4 + (g - 1) % 2][:, k * P:(k + 1) * P],
                                           e32[:, m % 2, (4 * c + k) * P:(4 * c + k + 1) * P], ident[:, :])
                    ins.then_inc(s_ptr, 1)

            def weighted_values(h, j):
                pe.wait_ge(s_ptl, 12 * h + TR[2 * j + 1])
                if j == 0:
                    pe.wait_ge(s_vl, h + 1)
                if not (isinstance(h, int) and h == 0 and j == 0):
                    pe.wait_ge(s_o, 4 * h + j)
                for k in range(2 * j + 2):
                    q = slice(P if k == 2 * j + 1 else 0, 2 * P)
                    for i, (v, pt) in enumerate(((v_hi, pt_hi), (v_hi, pt_lo), (v_lo, pt_hi))):
                        ins = pe.matmul(ps[6][:, q], v[:, k, :], pt[:, k, q], start=k == 0 and i == 0,
                                        stop=k == 2 * j + 1 and i == 2)
                ins.then_inc(s_pv, 1)

            def head(h, u, first, last):
                for m in range(NT):
                    scores(h, u, m)
                    if not (first and m < 2):
                        if m in (0, 2) and not first:
                            weighted_values(h - 1, 2 + m // 2)
                        if m in (4, 6):
                            weighted_values(h, m // 2 - 2)
                        transposes(*((h, m - 2) if m >= 2 else (h - 1, m + 6)))
                    if not last:
                        if m in (1, 3):
                            key_rms(h + 1, m // 2)
                        if m in (5, 6):
                            query_part(h + 1, m - 5)

            def attention():
                for f in range(2):
                    key_rms(0, f)
                for f in range(2):
                    query_part(0, f)
                head(0, 0, True, False)
                with pe.Fori(0, 3) as j:
                    for w in range(2):
                        head(2 * j + 1 + w, 1 - w, False, False)
                head(NH - 1, 1, False, True)
                weighted_values(NH - 1, 2)
                transposes(NH - 1, 6)
                transposes(NH - 1, 7)
                weighted_values(NH - 1, 3)

            def output_projection():
                pe.wait_ge(s_ol, NH)
                pe.wait_ge(s_o, 4 * NH)
                for c in range(NCH):
                    u, dt, f = c // 4, (c // 2) % 2, c % 2
                    if c % 4 == 0:
                        pe.wait_ge(s_wol, u + 1)
                    if c >= 4:
                        pe.wait_ge(s_ox, c - 3)
                    cols = slice(dt * P, (dt + 1) * P)
                    three(ps[4 + c % 4][:, :], [(wo_hi[:, u % 2, k, cols], wo_lo[:, u % 2, k, cols], hi_x[:, k, half(f)],
                                                 lo_x[:, k, half(f)]) for k in range(NH)]).then_inc(s_omm, 1)

            pe.wait_ge(s_xadd, 16)
            norm(0, 0)
            ffn(0)
            if stage == 2:
                norm(1, 1)
                ffn(1)
            if stage >= 3:
                latents()
                heads()
                attention()
                output_projection()
                norm(2, 1)
                ffn(1)
            pe.wait_ge(s_xadd, NCH * (1 + NG * min(stage, 2)))
            for t in range(NT):
                if t >= 2:
                    pe.wait_ge(s_oev, t - 1)
                    pe.wait_ge(s_oev2, t - 1)
                for b in range(2):
                    for k in range(4):
                        ins = pe.transpose(ps[4 + 2 * (t % 2) + b][:, k * P:(k + 1) * P],
                                           xT[:, 4 * b + k, t * P:(t + 1) * P], ident[:, :])
                    ins.then_inc(s_otr, 1)


_INS = ["x", "positions", "ln_mix_a", "w_pool", "b_pool", "pool_scale", "ln_ffn", "w_gate", "w_up", "w_down",
        "ln_kv", "w_dkv", "g_kv_latent", "w_uk", "w_uv", "g_k", "ln_mix_b", "w_dq", "g_q_latent", "w_uq", "g_q", "w_o"]


def kernel(**inputs):
    import concourse.bacc as bacc
    from concourse.bass_utils import run_bass_kernel_spmd

    nc = bacc.Bacc("TRN2", target_bir_lowering=False, num_devices=1)
    arrays, aps = {}, {}
    for name in _INS:
        v = np.ascontiguousarray(inputs[name])
        arrays[f"in_{name}"] = v
        aps[name] = nc.dram_tensor(f"in_{name}", v.shape, mybir.dt.from_np(v.dtype), kind="ExternalInput").ap()
    shape = inputs["x"].shape
    out = nc.dram_tensor("out_x", shape, mybir.dt.float32, kind="ExternalOutput").ap()
    build_trunk(nc, aps, out)
    r = run_bass_kernel_spmd(nc, [arrays], core_ids=[0])
    return r.results[0]["out_x"]
```

```python
import math

import numpy as np
import concourse.bass as bass
from concourse import mybir
from contextlib import ExitStack


def build_trunk(nc, a, out):
    F = mybir.dt.float32
    R = mybir.dt.float32r
    ALU = mybir.AluOpType
    ACT = mybir.ActivationFunctionType
    AX = mybir.AxisListType

    P = 128
    T, D = a["x"].shape[1:]
    FF = a["w_gate"].shape[2]
    KD = D // P
    NT = T // P
    HT = 512
    NF = FF // P
    NG = NF // 2
    NCH = 2 * KD
    EPS = 1e-6
    WINDOWS = (2, 4, 8, 16)
    KB = 1024
    BASE = 1152
    RL = a["w_dkv"].shape[1]
    KVR = a["g_kv_latent"].shape[0]
    QR = a["g_q_latent"].shape[1]
    ROPE = RL - KVR
    HR = ROPE // 2
    QKD = a["g_k"].shape[0]
    NOPE = QKD - ROPE
    NH = a["w_uq"].shape[2] // QKD
    KC, KQ = KVR // P, QR // P
    CW = RL + QR
    SCALE = 1.0 / math.sqrt(QKD)
    CHUNK = 64
    NEG = -1e30
    TWO_PI = 2.0 * math.pi
    MAGIC = 1.5 * 2.0 ** 23
    inv_freq = np.power(np.float32(10000.0), -np.arange(HR, dtype=np.float32) * np.float32(2.0) / np.float32(ROPE))

    def pieces(v, n):
        got = []
        for _ in range(n):
            e = math.floor(math.log2(abs(v)))
            q = 2.0 ** (e - 11)
            got.append(math.floor(v / q) * q)
            v -= got[-1]
        return got

    ctx = ExitStack()
    with ctx:
        def at(name, shape, dt, offset):
            return nc.alloc_sbuf_tensor_at(name, shape, dt, offset=BASE + int(offset))

        def sem(name):
            return ctx.enter_context(nc.semaphore(name))

        xT = at("xT", [P, KD, T], F, 0)
        hi_x = at("hi_x", [P, KD, T], R, 32 * KB)
        lo_x = at("lo_x", [P, KD, T], R, 64 * KB)
        gu_hi = at("gu_hi", [P, 2, 2 * KD, P], R, 96 * KB)
        gu_lo = at("gu_lo", [P, 2, 2 * KD, P], R, 112 * KB)
        a_hi = at("a_hi", [P, 2, 2, T], R, 128 * KB)
        a_lo = at("a_lo", [P, 2, 2, T], R, 144 * KB)
        wd_hi = at("wd_hi", [P, 2, D], R, 160 * KB)
        wd_lo = at("wd_lo", [P, 2, D], R, 168 * KB)
        raw_gu = at("raw_gu", [P, 2 * KD, 2 * P], F, 176 * KB)
        raw_wd = at("raw_wd", [P, D], F, 192 * KB)
        sil = at("sil", [P, 2, HT], F, 196 * KB)
        a32 = at("a32", [P, 2, HT], F, 200 * KB)
        rbc = at("rbc", [P, T], F, 204 * KB)
        sq = [at("sq0", [P, KD, HT], F, 196 * KB), at("sq1", [P, KD, HT], F, 144 * KB)]

        diag = at("diag", [P, 4, P], F, 212 * KB)
        y_tok = at("y_tok", [P, NT, D], F, 32 * KB)
        CB = 219 * KB
        ident = at("ident", [P, P], F, CB)
        ones = at("ones", [P, P], F, CB + 512)
        NROW = 64
        gT = at("gT", [P, NROW], F, CB + 1024)
        ss = at("ss", [P, NT], F, CB + 1280)
        rms = at("rms", [P, NT], F, CB + 1312)
        nhalf = at("nhalf", [P, 16], F, CB + 1344)
        bs = at("bs", [P, KD], F, CB + 1408)
        xtok = at("xtok", [P, NT, D], F, 128 * KB)
        wp_raw = at("wp_raw", [P, KD, 2 * P], F, 120 * KB)
        wp_hi = at("wp_hi", [P, KD, 2 * P], R, 160 * KB)
        wp_lo = at("wp_lo", [P, KD, 2 * P], R, 168 * KB)
        NW = len(WINDOWS)
        WMAX = WINDOWS[-1]
        band = at("band", [P, 2, NW, P], F, 196 * KB)
        band_t = at("band_t", [P, NW, WMAX], F, 200 * KB)
        grow = at("grow", [NROW, P], F, 201 * KB)
        invc = at("invc", [P, WMAX], F, 202 * KB)
        sqt = at("sqt", [P, D], F, 204 * KB)
        ytmp = at("ytmp", [P, 2, HT], F, 104 * KB)
        cos_t = at("cos_t", [P, NT, HR], F, CB + 1536)
        sin_t = at("sin_t", [P, NT, HR], F, CB + 2560)
        tab = at("tab", [P, 4, NT, HR], F, 214 * KB)
        pos_i = at("pos_i", [NT, P], mybir.dt.int32, 218 * KB)
        pos_row = at("pos_row", [NT, P], F, 218 * KB + 512)
        pos_f = at("pos_f", [P, NT], F, CB + 3584)
        inv_t = at("inv_t", [P, HR], F, CB + 3616)
        halfpi = at("halfpi", [P, 1], F, CB + 3744)
        wc_hi = [at(f"wc_hi{k}", [P, CW], R, 96 * KB + 4 * CW * k) for k in range(KD)]
        wc_at = (122 * KB, 136 * KB, 136 * KB + 4 * CW, 152 * KB, 152 * KB + 4 * CW,
                 208 * KB, 208 * KB + 4 * CW, 208 * KB + 8 * CW)
        wc_lo = [at(f"wc_lo{k}", [P, CW], R, wc_at[k]) for k in range(KD)]
        raw_c = at("raw_c", [P, 4, CW], F, 176 * KB)
        junk = at("junk", [P, CW], F, 189 * KB)

        def csq(h, k):
            return (csq0[:, k if k < 7 else 1, :], (csq1, csq2)[k // 4][:, k % 4, :])[h]

        csq0 = at("csq0", [P, 7, HT], F, 194 * KB)
        csq1 = at("csq1", [P, 4, HT], F, 128 * KB)
        csq2 = at("csq2", [P, 4, HT], F, 144 * KB)
        c_tok = at("c_tok", [P, 2, KVR + QR], F, 196 * KB)
        cT_hi = at("cT_hi", [P, KC, T], R, 0)
        cT_lo = at("cT_lo", [P, KC, T], R, 16 * KB)
        cqT_hi = at("cqT_hi", [P, KQ, T], R, 160 * KB)
        cqT_lo = at("cqT_lo", [P, KQ, T], R, 168 * KB)
        kpe = at("kpe", [P, NT, ROPE], F, 202 * KB)
        g_rope = at("g_rope", [P, 2, ROPE], F, 192 * KB + 512)
        ssl = at("ssl", [P, NT, 2], F, 193 * KB)
        rl = at("rl", [P, NT, 2], F, 193 * KB + 64)
        ssqpe = at("ssqpe", [P, NH, NT], F, 193 * KB + 128)
        sskpe = at("sskpe", [P, NT], F, CB + 3840)
        gkq = at("gkq", [P, 1], F, CB + 3872)
        kn = at("kn", [P, NH, T], F, 32 * KB)
        qn = at("qn", [P, NH, T], F, 64 * KB)
        v32 = at("v32", [P, NT, NH * P], F, 96 * KB)
        qpe = [at("qpe0", [P, 4, NH, ROPE], F, 136 * KB), at("qpe1", [P, 4, NH, ROPE], F, 152 * KB)]
        krT = at("krT", [P, T], F, 196 * KB)
        kg = at("kg", [P, NT, ROPE], F, 32 * KB)
        krt = at("krt", [P, 2, NT, HR], F, 34 * KB)
        krd = at("krd", [P, NT, 2, ROPE], F, 36 * KB)
        dsq = at("dsq", [P, 2, HT], F, 204 * KB)
        rt = at("rt", [P, 4, 2, 4, HR], F, 184 * KB)
        qsq = at("qsq", [P, 2, 4, ROPE], F, 188 * KB)
        qg = at("qg", [P, 2, 4, ROPE], F, 190 * KB)
        dw_raw = at("dw_raw", [P, 2, 4, 2 * P], F, 176 * KB)
        dw_hi = at("dw_hi", [P, 2, 4, 2 * P], R, 128 * KB)
        dw_lo = at("dw_lo", [P, 2, 4, 2 * P], R, 144 * KB)
        rk = at("rk", [P, NH, NT], F, CB + 3584)
        rq = at("rq", [P, NH, NT], F, CB + 1536)
        nrq = at("nrq", [P, NH, NT], F, CB + 1792)
        mx = at("mx", [P, 2], F, CB + 2048)
        nb = at("nb", [P, 2], F, CB + 2080)
        esum = at("esum", [P, 2], F, CB + 2112)
        rsum = at("rsum", [P, 2], F, CB + 2144)
        def pair(name, places):
            return [at(f"{name}{i}", [P, T], R, place * KB) for i, place in enumerate(places)]

        khi = pair("khi", (184, 28))
        klo = at("klo", [P, NH, T], R, 32 * KB)
        kr1 = pair("kr1", (188, 128))
        kr2 = pair("kr2", (200, 132))
        qs = pair("qs", (208, 144))
        qhi = pair("qhi", (160, 148))
        qlo = pair("qlo", (164, 176))
        v_hi = at("v_hi", [P, NT, P], R, 168 * KB)
        v_lo = at("v_lo", [P, NT, P], R, 172 * KB)
        pt_hi = at("pt_hi", [P, NT, 2 * P], R, 0)
        pt_lo = at("pt_lo", [P, NT, 2 * P], R, 8 * KB)
        e32 = at("e32", [P, 3, T], F, 16 * KB)
        krs = at("krs", [P, HT], F, 212 * KB)
        kdiag = at("kdiag", [P, 4, P], F, 214 * KB)
        qhl = at("qhl", [P, NT, 2, ROPE], R, 192 * KB)
        wo_raw = [at("wo_raw0", [P, NH, 2 * P], F, 136 * KB), at("wo_raw1", [P, NH, 2 * P], F, 152 * KB)]
        wo_hi = [at("wo_hi0", [P, NH, 2 * P], R, 104 * KB), at("wo_hi1", [P, NH, 2 * P], R, 160 * KB)]
        wo_lo = [at("wo_lo0", [P, NH, 2 * P], R, 120 * KB), at("wo_lo1", [P, NH, 2 * P], R, 168 * KB)]

        PS = ctx.enter_context(nc.psum_tensor("banks", [P, 8, 512], F))
        ps = [PS[:, i, :] for i in range(8)]
        ps_scores = [PS[:, 2 * i:2 * i + 2, :].rearrange("p b c -> p (b c)") for i in range(2)]

        ROW = {}
        at_row = 0
        for name, n in (("ln_mix_a", 8), ("pool_scale", 8), ("b_pool", 8), ("ln_ffn0", 8), ("ln_ffn1", 8),
                        ("ln_kv", 8), ("ln_mix_b", 8), ("g_kv_latent", 4), ("g_q_latent", 2), ("g_k", 1), ("g_q", 1)):
            ROW[name] = at_row
            at_row += n
        assert at_row == NROW

        def gain(name, k):
            return gT[:, ROW[name] + k:ROW[name] + k + 1]

        g_src = [("ln_mix_a", a["ln_mix_a"][0, :], 8), ("pool_scale", a["pool_scale"][0, :], 8),
                 ("b_pool", a["b_pool"][0, :, :].rearrange("g c -> (g c)"), 8),
                 ("ln_ffn0", a["ln_ffn"][0, :], 8), ("ln_ffn1", a["ln_ffn"][1, :], 8), ("ln_kv", a["ln_kv"], 8),
                 ("ln_mix_b", a["ln_mix_b"][0, :], 8), ("g_kv_latent", a["g_kv_latent"], 4),
                 ("g_q_latent", a["g_q_latent"][0, :], 2), ("g_k", a["g_k"][0:P], 1), ("g_q", a["g_q"][0, 0:P], 1)]

        s_x = [sem(f"x_in{t}") for t in range(NT)]
        s_g = sem("gains_in")
        s_wp = sem("w_pool_in")
        s_const = sem("constants")
        s_gT = sem("gains_transposed")
        s_gc = sem("gains_copied")
        s_bs = sem("bias_scaled")
        s_xtr = sem("x_transposed")
        s_xev = sem("x_evacuated")
        s_ssA = sem("square_sums_a")
        s_pool1 = sem("pool_steps")
        s_rA = sem("rms_a")
        s_xs = sem("x_scaled")
        s_windows = sem("windows")
        s_band = sem("bands")
        s_rope = sem("rope_constants")
        s_dmmA = sem("pool_d_products")
        s_dve = sem("vector_steps")
        s_dhi = sem("pool_d_hi")
        s_dlo = sem("pool_d_lo")
        s_wph = sem("w_pool_hi")
        s_wpl = sem("w_pool_lo")
        s_py = sem("pool_y")
        s_rgu = sem("gate_up_in")
        s_rwd = sem("down_in")
        s_guh = sem("gate_up_hi")
        s_gul = sem("gate_up_lo")
        s_wdh = sem("down_hi")
        s_wdl = sem("down_lo")
        s_gumm = sem("gate_up_products")
        s_sil = sem("silu_done")
        s_a32 = sem("a_done")
        s_ahi = sem("a_hi_done")
        s_alo = sem("a_lo_done")
        s_dmm = sem("residual_products")
        s_xadd = sem("x_added")
        s_sq = sem("squares")
        s_sqs = sem("squares_summed_over_tiles")
        s_ssm = sem("square_sum_products")
        s_ss = sem("square_sums")
        s_r = sem("rms")
        s_dg = sem("diag")
        s_bc = sem("rms_broadcast")
        s_rbc = sem("rms_broadcast_copied")
        s_hhi = sem("h_hi_done")
        s_hlo = sem("h_lo_done")
        s_gr1 = sem("gates_scaled")
        s_ar = sem("a_scaled")
        s_pos = sem("positions_in")
        s_posf = sem("positions_float")
        s_posc = sem("positions_copied")
        s_posT = sem("positions_transposed")
        s_ang = sem("angles_reduced")
        s_tab = sem("rope_tables")
        s_spill = [sem(f"x_spilled{h}") for h in range(2)]
        s_cr = [sem(f"latent_weights_in{i}") for i in range(4)]
        s_gr = sem("rope_gains_in")
        s_wch = sem("latent_weights_hi")
        s_wcl = sem("latent_weights_lo")
        s_xch = sem("x_hi_latent")
        s_xcl = sem("x_lo_latent")
        s_cmm = sem("latent_products")
        s_xsq = sem("x_squares")
        s_xadds = sem("x_squares_added")
        s_xsm = sem("x_square_sum_products")
        s_csq = sem("latent_square_sums")
        s_rl = sem("latent_rms")
        s_ctok = sem("latents_normed")
        s_ctr = sem("latents_transposed")
        s_chi = sem("latents_hi")
        s_clo = sem("latents_lo")
        s_krd = sem("key_part_rotated")
        s_krtr = sem("key_part_transposed")
        s_krT = sem("key_part_ready")
        s_dwr = [sem(f"head_weights_in{i}") for i in range(2)]
        s_dwh = sem("head_weights_hi")
        s_dwl = sem("head_weights_lo")
        s_vmm = sem("value_products")
        s_vev = sem("values_evacuated")
        s_veva = sem("values_evacuated_by_act")
        s_kmm = sem("head_products")
        s_kev = sem("heads_evacuated")
        s_ksq = sem("head_squares")
        s_kst = sem("head_square_sums")
        s_kstc = sem("head_sums_copied")
        s_rk = sem("head_rms")
        s_qrmm = sem("query_part_products")
        s_qsq = sem("query_part_squares")
        s_qg = sem("query_part_gained")
        s_qcs = sem("query_part_crossed")
        s_qpe = sem("query_part_rotated")
        s_rqs = sem("query_scales")
        s_kd = sem("key_rms_diag")
        s_kbc = sem("key_rms_broadcast")
        s_kf = sem("keys_scaled")
        s_khi = sem("keys_hi")
        s_klo = sem("keys_lo")
        s_qh = sem("queries_hi")
        s_ql = sem("queries_lo")
        s_qhl = sem("query_part_split")
        s_qtr = sem("query_part_transposed")
        s_qs = sem("query_part_ready")
        s_vh = sem("values_hi")
        s_vl = sem("values_lo")
        s_sc = sem("scores")
        s_mask = sem("scores_masked")
        s_max = sem("row_maxima")
        s_nb = sem("exp_biases")
        s_exp = sem("exponentials")
        s_rs = sem("row_sums_inverted")
        s_p = sem("probabilities")
        s_ptr = sem("probabilities_transposed")
        s_pth = sem("probabilities_hi")
        s_ptl = sem("probabilities_lo")
        s_pv = sem("attention_products")
        s_o = sem("attention_out")
        s_back = [sem(f"x_back{k}") for k in range(KD)]
        s_wor = [sem(f"w_o_in{i}") for i in range(2)]
        s_woh = sem("w_o_hi")
        s_wol = sem("w_o_lo")
        s_oh = sem("o_hi")
        s_ol = sem("o_lo")
        s_omm = sem("w_o_products")
        s_ox = sem("x_attention_added")
        s_otr = sem("out_transposed")
        s_oev = sem("out_first_half")
        s_oev2 = sem("out_second_half")
        s_out = sem("out_written")

        x_in = a["x"][0, :, :].rearrange("(t p) d -> t p d", p=P)
        x_out = out[0, :, :].rearrange("(t p) d -> t p d", p=P)
        wdkv_v = a["w_dkv"].rearrange("(k p) c -> p k c", p=P)
        wdq_v = a["w_dq"][0, :, :].rearrange("(k p) c -> p k c", p=P)
        wuk_v = a["w_uk"].rearrange("(k p) c -> p k c", p=P)
        wuv_v = a["w_uv"].rearrange("(k p) c -> p k c", p=P)
        wuq_v = a["w_uq"][0, :, :].rearrange("(k p) (h c) -> p k h c", p=P, c=QKD)
        wo_v = a["w_o"][0, :, :].rearrange("(k p) c -> p k c", p=P)
        x_mid = nc.dram_tensor("x_mid", (P, KD, T), F, kind="Internal").ap()
        wg_v = [a["w_gate"][l, :, :].rearrange("(k p) f -> p k f", p=P) for l in range(2)]
        wu_v = [a["w_up"][l, :, :].rearrange("(k p) f -> p k f", p=P) for l in range(2)]
        wd_v = [a["w_down"][l, :, :].rearrange("(f p) d -> f p d", p=P) for l in range(2)]

        NCONST = 3
        NROPE = HR + 1

        UNITS = [("rotated", 0, KQ), ("values", 0, KC), ("rotated", 1, KQ), ("values", 1, KC), ("values", 2, KC),
                 ("values", 3, KC)] + [("queries", n, KQ) for n in range(4)] + [("keys", n, KC) for n in range(4)]

        def unit_done(u):
            kind, n, _ = UNITS[u]
            return {"rotated": (s_qrmm, 4 * n + 4), "values": (s_vmm, 8 * n + 8), "queries": (s_kmm, 4 * n + 4),
                    "keys": (s_kmm, 4 * n + 20)}[kind]

        def unit_arrived(u):
            return sum(16 * (1 if UNITS[i][2] == KC else KQ) for i in range(u % 2, u + 1, 2))

        def unit_gain(u):
            return "g_kv_latent" if UNITS[u][2] == KC else "g_q_latent"

        ORDER = (0, 1, 6, 7, 2, 3, 4, 5)
        TR = [sum(m // 4 + 1 for m in ORDER[:i + 1]) for i in range(NT)]

        def banks_of(i):
            m = ORDER[i]
            return [(c, TR[i] - m // 4 + c, min(4, m + 1 - 4 * c)) for c in range(m // 4 + 1)]

        def table(t, n):
            return t[:, 2 * n:2 * n + 2, :].unsqueeze(2).broadcast_to([P, 2, 4, HR])

        def half(h):
            return slice(h * HT, (h + 1) * HT)

        def pool_d_banks(t):
            first = 2 + 2 * (t % 2)
            return PS[:, first:first + 2, :].rearrange("p b (k t) -> p (b k) t", t=P)

        def wait_x(e, l, h, k):
            if l == 0:
                e.wait_ge(s_xadd, KD * h + k + 1)
            else:
                e.wait_ge(s_ox, 4 * (k // 2) + 2 * h + k % 2 + 1)

        block = ctx.enter_context(nc.Block())

        @block.sync
        def _(sp):
            for t in range(NT):
                sp.dma_start(xtok[:, t, :], x_in[t, :, :]).then_inc(s_x[t], 16)
                if t == 1:
                    sp.dma_start(pos_i[:, :], a["positions"][0, :].rearrange("(t p) -> t p", p=P)).then_inc(s_pos, 16)
                    for name, src, n in g_src:
                        sp.dma_start(grow[ROW[name]:ROW[name] + n, :], src.rearrange("(k p) -> k p", p=P)).then_inc(s_g, 16)
                    sp.dma_start(wp_raw[:, :, :], a["w_pool"][0, :, :, :].rearrange("g (k p) d -> p (g k) d", p=P)).then_inc(s_wp, 16)

            def load_gate_up(l, i):
                g = l * NG + i
                if not (isinstance(g, int) and g == 0):
                    sp.wait_ge(s_gul, 2 * g)
                sp.dma_start(raw_gu[:, 0:KD, :], wg_v[l][:, :, bass.ds(i * 2 * P, 2 * P)]).then_inc(s_rgu, 16)
                sp.dma_start(raw_gu[:, KD:2 * KD, :], wu_v[l][:, :, bass.ds(i * 2 * P, 2 * P)]).then_inc(s_rgu, 16)

            def load_down(l, f):
                n = l * NF + f
                if not (isinstance(n, int) and n == 0):
                    sp.wait_ge(s_wdl, n)
                sp.dma_start(raw_wd[:, :], wd_v[l][f, :, :]).then_inc(s_rwd, 16)

            def ffn(l):
                load_gate_up(l, 0)
                load_down(l, 0)
                load_gate_up(l, 1)
                for i in range(NG - 2):
                    load_down(l, 2 * i + 1)
                    load_gate_up(l, i + 2)
                    load_down(l, 2 * i + 2)
                load_down(l, NF - 3)
                load_down(l, NF - 2)
                load_down(l, NF - 1)

            ffn(0)
            sp.wait_ge(s_gul, NF)
            for k in range(KD):
                if k >= 4:
                    sp.wait_ge(s_wcl, k - 3)
                sp.dma_start(raw_c[:, k % 4, 0:RL], wdkv_v[:, k, :]).then_inc(s_cr[k % 4], 16)
                sp.dma_start(raw_c[:, k % 4, RL:CW], wdq_v[:, k, :]).then_inc(s_cr[k % 4], 16)
            for h in range(2):
                sp.wait_ge(s_xadd, NCH * NG + KD * (h + 1))
                sp.dma_start(x_mid[:, :, half(h)], xT[:, :, half(h)]).then_inc(s_spill[h], 16)
            sp.dma_start(g_rope[:, 0, :], a["g_k"][NOPE:QKD].partition_broadcast(P)).then_inc(s_gr, 16)
            sp.dma_start(g_rope[:, 1, :], a["g_q"][0, NOPE:QKD].partition_broadcast(P)).then_inc(s_gr, 16)
            sp.wait_ge(s_wcl, KD)
            for u, (kind, n, nk) in enumerate(UNITS):
                if u >= 2:
                    sp.wait_ge(s_dwl, u - 1)
                raw, done = dw_raw[:, u % 2, :, :], s_dwr[u % 2]
                if kind == "values":
                    sp.dma_start(raw, wuv_v[:, :, 2 * P * n:2 * P * (n + 1)]).then_inc(done, 16)
                elif kind == "keys":
                    sp.dma_start(raw, wuk_v[:, :, 2 * P * n:2 * P * (n + 1)]).then_inc(done, 16)
                else:
                    for k in range(KQ):
                        if kind == "rotated":
                            src = wuq_v[:, k, 4 * n:4 * n + 4, NOPE:QKD]
                        else:
                            src = wuq_v[:, k, 2 * n:2 * n + 2, 0:NOPE]
                        sp.dma_start(raw[:, k, :].rearrange("p (h c) -> p h c", h=src.shape[1]), src).then_inc(done, 16)
            sp.wait_ge(s_qtr, 2 * NH)
            for u in range(4):
                if u >= 2:
                    sp.wait_ge(s_wol, u - 1)
                sp.dma_start(wo_raw[u % 2][:, :, :], wo_v[:, :, 2 * P * u:2 * P * (u + 1)]).then_inc(s_wor[u % 2], 16)
                if u == 1:
                    sp.wait_ge(s_pv, 4 * NH)
                    for h in range(2):
                        sp.wait_ge(s_spill[h], 16)
                    for k in range(KD):
                        sp.dma_start(xT[:, k, :], x_mid[:, k, :]).then_inc(s_back[k], 16)
            ffn(1)
            for t in range(NT):
                sp.wait_ge(s_oev, t + 1)
                sp.wait_ge(s_oev2, t + 1)
                sp.dma_start(x_out[t, :, :], y_tok[:, t, :]).then_inc(s_out, 16)
            sp.wait_ge(s_out, 16 * NT)

        @block.gpsimd
        def _(pool):
            steps1 = [0]

            def link(ins):
                steps1[0] += 1
                ins.then_inc(s_pool1, 1)
                pool.wait_ge(s_pool1, steps1[0])

            link(pool.memset(ident[:, :], 0.0))
            pool.affine_select(out=ident[:, :], in_=ident[:, :], compare_op=ALU.not_equal, fill=1.0, base=0,
                               pattern=[[-1, P]], channel_multiplier=1).then_inc(s_const, 1)
            pool.memset(ones[:, :], 1.0).then_inc(s_const, 1)
            pool.memset(nhalf[:, :], -0.5).then_inc(s_const, 1)
            for j in range(WMAX):
                pool.memset(invc[:, j:j + 1], 1.0 / (j + 1))
            for g, w in enumerate(WINDOWS):
                pool.memset(band_t[:, g, :], 1.0 / w)
                ins = pool.memset(band[:, :, g, :], 1.0 / w)
            link(ins)
            for g, w in enumerate(WINDOWS):
                ins = pool.tensor_copy(band[:, 0, g, 0:w], invc[:, 0:w])
                pool.affine_select(out=band_t[:, g, :], in_=band_t[:, g, :], compare_op=ALU.is_ge, fill=0.0,
                                   base=w - 1 - P, pattern=[[-1, WMAX]], channel_multiplier=1)
            link(ins)
            for g, w in enumerate(WINDOWS):
                ins = pool.affine_select(out=band[:, :, g, :], in_=band[:, :, g, :], compare_op=ALU.is_ge, fill=0.0,
                                         base=0, pattern=[[0, 2], [1, P]], channel_multiplier=-1)
            link(ins)
            for g, w in enumerate(WINDOWS):
                ins = pool.affine_select(out=band[:, :, g, :], in_=band[:, :, g, :], compare_op=ALU.is_ge, fill=0.0,
                                         base=w - 1, pattern=[[0, 2], [-1, P]], channel_multiplier=1)
            ins.then_inc(s_windows, 1)

            for t in range(NT):
                pool.wait_ge(s_ssA, t + 1)
                link(pool.tensor_scalar(rms[:, t:t + 1], ss[:, t:t + 1], 1.0 / D, EPS, ALU.mult, ALU.add))
                pool.tensor_tensor(rms[:, t:t + 1], rms[:, t:t + 1], nhalf[:, 0:1], ALU.pow).then_inc(s_rA, 1)
                if t == 0:
                    pool.wait_ge(s_pos, 16)
                    pool.tensor_copy(pos_row[:, :], pos_i[:, :]).then_inc(s_posf, 1)
            for j in range(HR):
                pool.memset(inv_t[:, j:j + 1], float(inv_freq[j])).then_inc(s_rope, 1)
            pool.memset(halfpi[:, :], math.pi / 2).then_inc(s_rope, 1)
            pool.wait_ge(s_rope, NROPE)
            pool.wait_ge(s_posc, 1)

            ang, whole, big, part_turn = (tab[:, i, :, :] for i in range(4))
            link(pool.tensor_tensor(ang, pos_f[:, :].unsqueeze(2).broadcast_to([P, NT, HR]),
                                    inv_t[:, :].unsqueeze(1).broadcast_to([P, NT, HR]), ALU.mult))
            link(pool.tensor_scalar(whole, ang, 1.0 / TWO_PI, MAGIC, ALU.mult, ALU.add))
            link(pool.tensor_scalar(whole, whole, MAGIC, None, ALU.subtract))
            link(pool.tensor_scalar(big, whole, MAGIC * 2048, None, ALU.add))
            link(pool.tensor_scalar(big, big, MAGIC * 2048, None, ALU.subtract))
            link(pool.tensor_tensor(whole, whole, big, ALU.subtract))
            for c in pieces(TWO_PI, 4):
                for turns in (big, whole):
                    link(pool.tensor_scalar(part_turn, turns, -c, None, ALU.mult))
                    link(pool.tensor_tensor(ang, ang, part_turn, ALU.add))
            link(pool.tensor_scalar(sin_t[:, :, :], ang, 3.1415925, -3.1415925, ALU.min, ALU.max))
            link(pool.tensor_scalar(big, sin_t[:, :, :], 0.0, 2.0, ALU.max, ALU.mult))
            pool.tensor_tensor(cos_t[:, :, :], big, sin_t[:, :, :], ALU.subtract).then_inc(s_ang, 1)
            pool.wait_ge(s_ang, 1)

            def stats(q, h):
                pool.wait_ge(s_ss, 2 * q + h + 1)
                part = rms[:, 4 * h:4 * h + 4]
                link(pool.tensor_scalar(part, ss[:, 4 * h:4 * h + 4], 1.0 / D, EPS, ALU.mult, ALU.add))
                pool.tensor_tensor(part, part, nhalf[:, 0:4], ALU.pow).then_inc(s_r, 1)

            def scale_gated(n, h):
                pool.wait_ge(s_a32, n + 1)
                pool.tensor_tensor(a32[:, h, :], a32[:, h, :], rbc[:, half(h)], ALU.mult).then_inc(s_ar, 1)

            def scale_tile(l, f):
                for h in range(2):
                    scale_gated(2 * (l * NF + f) + h, h)

            def ffn(l):
                for h in range(2):
                    for k in range(1, KD):
                        pool.wait_ge(s_sq, (2 * l + h) * KD + k + 1)
                        ins = pool.tensor_tensor(sq[h][:, 0, :], sq[h][:, 0, :], sq[h][:, k, :], ALU.add)
                        if k < KD - 1:
                            link(ins)
                    ins.then_inc(s_sqs, 1)
                    stats(2 * l, h)
                pool.wait_ge(s_rbc, 2 * l + 2)
                with pool.Fori(0, NG) as i:
                    for u in range(2):
                        scale_tile(l, 2 * i + u)

            ffn(0)

            def add_squares(h, k):
                pool.wait_ge(s_xsq, KD * h + k + 1)
                pool.tensor_tensor(csq(h, 0), csq(h, 0), csq(h, k), ALU.add).then_inc(s_xadds, 1)
                pool.wait_ge(s_xadds, (KD - 1) * h + k)

            for k in range(1, KD):
                add_squares(0, k)
            stats(1, 0)
            for t in range(NT):
                for k in ((1,), (2, 3, 4), (5, 6, 7))[t] if t < 3 else ():
                    add_squares(1, k)
                if t == 4:
                    stats(1, 1)
                pool.wait_ge(s_csq, t + 1)
                pool.tensor_scalar(rl[:, t, 0:1], ssl[:, t, 0:1], 1.0 / KVR, EPS, ALU.mult, ALU.add)
                link(pool.tensor_scalar(rl[:, t, 1:2], ssl[:, t, 1:2], 1.0 / QR, EPS, ALU.mult, ALU.add))
                pool.tensor_tensor(rl[:, t, :], rl[:, t, :], nhalf[:, 0:2], ALU.pow).then_inc(s_rl, 1)

            def head_rms(p):
                pool.wait_ge(s_kstc, p + 1)
                r = (rq, rk)[p // 4][:, 2 * (p % 4):2 * (p % 4) + 2, :].rearrange("p h t -> p (h t)")
                link(pool.tensor_scalar(r, r, 1.0 / QKD, EPS, ALU.mult, ALU.add))
                pool.tensor_tensor(r, r, nhalf[:, :], ALU.pow).then_inc(s_rk, 1)

            for n in range(8):
                pool.wait_ge(s_qg, n + 1)
                if n >= 1:
                    pool.wait_ge(s_qpe, n)
                pool.tensor_tensor(rt[:, 2, :, :, :], qg[:, :, :, HR:ROPE], table(cos_t, n % 4), ALU.mult)
                pool.tensor_tensor(rt[:, 3, :, :, :], qg[:, :, :, 0:HR], table(sin_t, n % 4), ALU.mult).then_inc(s_qcs, 1)
            for p in range(4):
                head_rms(p)

            def query_part(h):
                pool.wait_ge(s_qh, h + 1)
                for i in range(2):
                    ins = pool.tensor_tensor(qhl[:, 4 * i:4 * i + 4, 1, :], qpe[i][:, :, h, :],
                                             qhl[:, 4 * i:4 * i + 4, 0, :].bitcast(F), ALU.subtract)
                ins.then_inc(s_qhl, 1)

            def queries(h, u):
                pool.tensor_tensor(qlo[u][:, :], qn[:, h, :], qhi[u][:, :].bitcast(F), ALU.subtract).then_inc(s_ql, 1)

            def values(h):
                pool.wait_ge(s_vh, h + 1)
                pool.tensor_tensor(v_lo[:, :, :], v32[:, :, bass.ds(h * P, P)], v_hi[:, :, :].bitcast(F),
                                   ALU.subtract).then_inc(s_vl, 1)

            def keys(h, u, f):
                pool.wait_ge(s_khi, 2 * h + f + 1)
                pool.tensor_tensor(klo[:, h, half(f)], kn[:, h, half(f)], khi[u][:, half(f)].bitcast(F), ALU.subtract)
                pool.tensor_tensor(kr2[u][:, half(f)], krs[:, :], kr1[u][:, half(f)].bitcast(F),
                                   ALU.subtract).then_inc(s_klo, 1)

            def output_lo(h):
                pool.wait_ge(s_oh, h + 1)
                pool.tensor_tensor(lo_x[:, h, :], qn[:, h, :], hi_x[:, h, :].bitcast(F), ALU.subtract).then_inc(s_ol, 1)

            query_part(0)
            queries(0, 0)
            values(0)
            head_rms(4)
            head_rms(5)
            keys(0, 0, 0)
            keys(0, 0, 1)
            head_rms(6)
            head_rms(7)
            query_part(1)
            queries(1, 1)
            keys(1, 1, 0)
            keys(1, 1, 1)
            with pool.Fori(0, 3) as j:
                for w in range(2):
                    h = 2 * j + 1 + w
                    query_part(h + 1)
                    queries(h + 1, w)
                    values(h)
                    keys(h + 1, w, 0)
                    output_lo(h - 1)
                    keys(h + 1, w, 1)
            values(NH - 1)
            output_lo(NH - 2)
            output_lo(NH - 1)
            ffn(1)

        @block.scalar
        def _(act):
            def pool_d_hi(t):
                act.wait_ge(s_dmmA, t + 1)
                act.activation(hi_x[:, :, t * P:(t + 1) * P], pool_d_banks(t), ACT.Copy).then_inc(s_dhi, 1)

            def pool_y(n):
                k = n % KD
                act.wait_ge(s_dmm, n + 1)
                if n >= 2:
                    act.wait_ge(s_xadd, n - 1)
                act.activation(ytmp[:, n % 2, :], ps[6 + n % 2][:, :], ACT.Identity, scale=gain("pool_scale", k),
                               bias=bs[:, k:k + 1]).then_inc(s_py, 1)

            def mixer():
                for t in range(NT + 2):
                    if t < NT:
                        act.wait_ge(s_x[t], 16)
                        if t >= 1:
                            act.wait_ge(s_ssA, t)
                        act.activation(sqt[:, :], xtok[:, t, :], ACT.Square, accum_out=ss[:, t:t + 1]).then_inc(s_ssA, 1)
                    if t >= 2:
                        pool_d_hi(t - 2)
                    if t == 4:
                        act.wait_ge(s_wp, 16)
                        act.wait_ge(s_bs, 1)
                        for k in range(KD):
                            act.activation(wp_hi[:, k, :], wp_raw[:, k, :], ACT.Copy,
                                           scale=gain("ln_mix_a", k)).then_inc(s_wph, 1)
                    if t >= 7:
                        for n in range(2 * (t - 7), 2 * (t - 7) + 2):
                            pool_y(n)
                split_gate_up(0, 0, 0)
                for n in range(6, NCH):
                    pool_y(n)
                    if n >= KD:
                        x_high(0, 0, n - KD)

            def x_high(l, h, k):
                wait_x(act, l, h, k)
                if l == 0:
                    act.wait_ge(s_dmm, KD * h + 2 * (k // 2) + 2)
                else:
                    act.wait_ge(s_omm, NCH - 2 + 2 * h)
                act.activation(hi_x[:, k, half(h)], xT[:, k, half(h)], ACT.Copy,
                               scale=gain(f"ln_ffn{l}", k)).then_inc(s_hhi, 1)

            def norm(l):
                for h in range(2):
                    for k in range(KD):
                        if l == 1 or h == 1:
                            x_high(l, h, k)
                    if h == 0:
                        if l == 0:
                            act.wait_ge(s_xadd, NCH)
                        split_gate_up(l, 0, 1)
                    if h == 1 and l == 1:
                        act.wait_ge(s_wol, 4)
                    for k in range(KD):
                        act.activation(sq[h][:, k, :], xT[:, k, half(h)], ACT.Square).then_inc(s_sq, 1)

            def split_gate_up(l, i, u):
                g, n = l * NG + i, l * NF + 2 * i + u
                if u == 0:
                    act.wait_ge(s_rgu, 32 * g + 32)
                if not (isinstance(n, int) and n < 2):
                    act.wait_ge(s_gumm, 2 * n - 2)
                act.activation(gu_hi[:, u, :, :], raw_gu[:, :, u * P:(u + 1) * P], ACT.Copy).then_inc(s_guh, 1)

            def split_down(l, i, u):
                g, n = l * NG + i, l * NF + 2 * i + u
                act.wait_ge(s_rwd, 16 * n + 16)
                act.wait_ge(s_dmm, NCH * (g + 1))
                act.activation(wd_hi[:, u, :], raw_wd[:, :], ACT.Copy).then_inc(s_wdh, 1)

            def a_high(l, i, u, par, h):
                n = 2 * (l * NF + 2 * i + u) + h
                act.wait_ge(s_ar, n + 1)
                act.activation(a_hi[:, par, u, half(h)], a32[:, h, :], ACT.Copy).then_inc(s_ahi, 1)

            def gated(l, i, u, par, before, last=False):
                for h in range(2):
                    n = 2 * (l * NF + 2 * i + u) + h
                    act.wait_ge(s_gr1, n + 1)
                    act.activation(sil[:, h, :], sil[:, h, :], ACT.Silu).then_inc(s_sil, 1)
                    if before is not None:
                        a_high(l, *before)
                    before = (i, u, par, h)
                    if last:
                        a_high(l, *before)
                        before = None

            def body(l, i, par, last):
                if not last:
                    split_gate_up(l, i + 1, 0)
                split_down(l, i, 0)
                if last:
                    split_down(l, i, 1)
                gated(l, i, 1, par, (i, 0, par, 1), last)
                if not last:
                    split_gate_up(l, i + 1, 1)
                    split_down(l, i, 1)
                if not last:
                    gated(l, i + 1, 0, 1 - par, (i, 1, par, 1))

            def ffn(l):
                norm(l)
                if l == 0:
                    act.wait_ge(s_ang, 1)
                    act.activation(sin_t[:, :, :], sin_t[:, :, :], ACT.Sin)
                    act.activation(cos_t[:, :, :], cos_t[:, :, :], ACT.Sin, scale=-1.0, bias=halfpi[:, 0:1]).then_inc(s_tab, 1)
                gated(l, 0, 0, 0, None)
                with act.Fori(0, NG // 2) as j:
                    body(l, 2 * j, 0, False)
                    body(l, 2 * j + 1, 1, False)
                body(l, NG - 1, 0, True)

            def split_x(h, k):
                act.wait_ge(s_xadd, NCH * NG + KD * h + k + 1)
                act.activation(hi_x[:, k, half(h)], xT[:, k, half(h)], ACT.Copy).then_inc(s_xch, 1)

            def squares(h):
                if h == 1:
                    act.wait_ge(s_dmm, NCH * (NG + 1))
                for k in range(KD):
                    if h == 0 and k == 7:
                        act.wait_ge(s_xadds, 1)
                    act.activation(csq(h, k), xT[:, k, half(h)], ACT.Square).then_inc(s_xsq, 1)

            def latents():
                act.wait_ge(s_gumm, 2 * NF)
                for k in range(KD):
                    act.wait_ge(s_cr[k % 4], 32 * (k // 4 + 1))
                    act.activation(wc_hi[k][:, 0:RL], raw_c[:, k % 4, 0:RL], ACT.Copy, scale=gain("ln_kv", k))
                    act.activation(wc_hi[k][:, RL:CW], raw_c[:, k % 4, RL:CW], ACT.Copy,
                                   scale=gain("ln_mix_b", k)).then_inc(s_wch, 1)
                for k in range(KD):
                    split_x(0, k)
                act.wait_ge(s_alo, 2 * NF)
                squares(0)
                for k in range(KD):
                    split_x(1, k)
                squares(1)
                for t in range(NT):
                    b = 4 * (t % 2)
                    act.wait_ge(s_cmm, t + 1)
                    act.wait_ge(s_r, 2 + t // 4 + 1)
                    r = rms[:, t:t + 1]
                    if t >= 1:
                        act.wait_ge(s_csq, t)
                    act.activation(junk[:, 0:KVR], ps[b][:, 0:KVR], ACT.Square, scale=r, accum_out=ssl[:, t, 0:1])
                    act.activation(junk[:, KVR:RL], ps[b + 1][:, 0:ROPE], ACT.Square, scale=r, accum_out=sskpe[:, t:t + 1])
                    act.activation(junk[:, RL:CW], ps[b + 1][:, ROPE:ROPE + QR], ACT.Square, scale=r,
                                   accum_out=ssl[:, t, 1:2]).then_inc(s_csq, 1)
                    if t >= 1:
                        latent_hi(t - 1)
                    if t >= 6:
                        split_unit(t - 6)
                latent_hi(NT - 1)

            def latent_hi(t):
                act.wait_ge(s_ctr, t + 1)
                if t == 0:
                    for h in range(2):
                        act.wait_ge(s_spill[h], 16)
                    act.wait_ge(s_xcl, 2 * KD)
                tok = slice(t * P, (t + 1) * P)
                act.activation(cT_hi[:, :, tok], ps[6][:, :].rearrange("p (k t) -> p k t", t=P), ACT.Copy)
                act.activation(cqT_hi[:, :, tok], ps[7][:, 0:KQ * P].rearrange("p (k t) -> p k t", t=P),
                               ACT.Copy).then_inc(s_chi, 1)

            def split_unit(u):
                act.wait_ge(s_dwr[u % 2], unit_arrived(u))
                if u < 2:
                    act.wait_ge(s_xadds, 2 * (KD - 1))
                    act.wait_ge(s_xsm, 2)
                else:
                    act.wait_ge(*unit_done(u - 2))
                for k in range(UNITS[u][2]):
                    ins = act.activation(dw_hi[:, u % 2, k, :], dw_raw[:, u % 2, k, :], ACT.Copy, scale=gain(unit_gain(u), k))
                ins.then_inc(s_dwh, 1)

            def rotated_squares(n):
                act.wait_ge(s_qrmm, n + 1)
                if n >= 1:
                    act.wait_ge(s_qg, n)
                act.activation(qsq[:, :, :, :], ps[n % 4][:, :].rearrange("p (t h c) -> p t h c", t=2, c=ROPE),
                               ACT.Square).then_inc(s_qsq, 1)

            def evacuate_values(n, t):
                act.wait_ge(s_vmm, 8 * n + t + 1)
                act.activation(v32[:, t, n * 2 * P:(n + 1) * 2 * P], ps[4 + t % 4][:, 0:2 * P], ACT.Copy).then_inc(s_veva, 1)

            def head_squares(b):
                p = b // 4
                src = (qn, kn)[p // 4][:, 2 * (p % 4) + (b // 2) % 2, half(b % 2)]
                act.wait_ge(s_kev, b + 1)
                if b >= 2:
                    act.wait_ge(s_kst, b - 1)
                act.activation(dsq[:, b % 2, :], src, ACT.Square).then_inc(s_ksq, 1)

            def heads():
                for n in range(3):
                    rotated_squares(n)
                for n, t in ((n, t) for n in range(3) for t in range(NT)):
                    if t == 4:
                        if n == 0:
                            rotated_squares(3)
                        split_unit(2 * n + 2)
                    evacuate_values(n, t)
                    if t == NT - 1 and n < 2:
                        split_unit(2 * n + 3)
                        for i in (4, 5) if n == 0 else (6, 7):
                            rotated_squares(i)
                split_unit(7)
                for p in range(8):
                    for b in range(4 * p, 4 * p + 4):
                        head_squares(b)
                        if b == 22:
                            query_part(0, 0, 0, 0)
                            query_part(0, 0, 1, 1)
                        if b in (27, 30):
                            prepare_keys(0, 0, b // 30)
                    if p < 6:
                        split_unit(p + 8)
                    if p == 4:
                        prepare_queries(0, 0)

            def prepare_keys(h, u, f):
                act.wait_ge(s_kf, 2 * h + f + 1)
                act.activation(kr1[u][:, half(f)], krs[:, :], ACT.Copy)
                act.activation(khi[u][:, half(f)], kn[:, h, half(f)], ACT.Copy).then_inc(s_khi, 1)

            def prepare_queries(h, u):
                act.wait_ge(s_rqs, 1)
                for i in range(2):
                    act.activation(qhl[:, 4 * i:4 * i + 4, 0, :], qpe[i][:, :, h, :], ACT.Copy)
                act.activation(qhi[u][:, :], qn[:, h, :], ACT.Copy).then_inc(s_qh, 1)

            def query_part(h, u, f, bank=7):
                act.wait_ge(s_qtr, 2 * h + f + 1)
                act.activation(qs[u][:, half(f)], ps[bank][:, :], ACT.Copy).then_inc(s_qs, 1)

            def exponentials(h, i):
                n, m = h * NT + i, ORDER[i]
                w = (m + 1) * P
                act.wait_ge(s_nb, n + 1)
                if i >= 3:
                    act.wait_ge(s_ptr, 12 * h + TR[i - 3])
                elif not (isinstance(h, int) and h == 0):
                    act.wait_ge(s_ptr, 12 * h - 12 + TR[(6, 7, 5)[i]])
                act.wait_ge(s_rqs, 1)
                act.activation(e32[:, i % 3, 0:w], ps_scores[i % 2][:, 0:w], ACT.Exp, scale=rq[:, h, m:m + 1],
                               bias=nb[:, i % 2:i % 2 + 1], accum_out=esum[:, i % 2:i % 2 + 1]).then_inc(s_exp, 1)

            def probabilities(h, i):
                w = (ORDER[i] + 1) * P
                act.wait_ge(s_rs, h * NT + i + 1)
                act.activation(e32[:, i % 3, 0:w], e32[:, i % 3, 0:w], ACT.Copy,
                               scale=rsum[:, i % 2:i % 2 + 1]).then_inc(s_p, 1)

            def transposed_hi(h, i):
                if i % 2 == 0 and not (isinstance(h, int) and h == 0 and i == 0):
                    act.wait_ge(s_pv, 4 * h + i // 2)
                for c, g, count in banks_of(i):
                    act.wait_ge(s_ptr, 12 * h + g)
                    act.activation(pt_hi[:, 4 * c:4 * c + count, (i % 2) * P:(i % 2 + 1) * P],
                                   ps[4 + (g - 1) % 2][:, 0:count * P].rearrange("p (k q) -> p k q", q=P),
                                   ACT.Copy).then_inc(s_pth, 1)

            def out_tile(h, j):
                at_token = ORDER[2 * j] * P
                act.activation(qn[:, h, at_token:at_token + 2 * P], ps[6][:, 0:2 * P], ACT.Copy).then_inc(s_o, 1)

            def output_hi(h):
                act.activation(hi_x[:, h, :], qn[:, h, :], ACT.Copy).then_inc(s_oh, 1)

            def head(h, u, first, last):
                for m in range(NT):
                    if not (first and m < 2):
                        transposed_hi(*((h, m - 2) if m >= 2 else (h - 1, m + 6)))
                    if m == 3 and not first:
                        act.wait_ge(s_o, 4 * h)
                    if not (first and m == 0):
                        probabilities(*((h, m - 1) if m >= 1 else (h - 1, 7)))
                    if m == 3 and not first:
                        output_hi(h - 1)
                    exponentials(h, m)
                    if m in (0, 2) and not first:
                        out_tile(h - 1, 2 + m // 2)
                    if m in (4, 6):
                        out_tile(h, m // 2 - 2)
                    if not last:
                        if m == 1:
                            prepare_queries(h + 1, 1 - u)
                        if m in (2, 4):
                            prepare_keys(h + 1, 1 - u, m // 2 - 1)
                        if m in (5, 6):
                            query_part(h + 1, 1 - u, m - 5)
                    elif m == 5:
                        split_wo(0)

            def attention():
                head(0, 0, True, False)
                with act.Fori(0, 3) as j:
                    for w in range(2):
                        head(2 * j + 1 + w, 1 - w, False, False)
                head(NH - 1, 1, False, True)
                probabilities(NH - 1, 7)
                transposed_hi(NH - 1, 6)
                out_tile(NH - 1, 2)
                transposed_hi(NH - 1, 7)
                act.wait_ge(s_pv, 4 * NH)
                out_tile(NH - 1, 3)

            def output_projection():
                act.wait_ge(s_o, 4 * NH)
                output_hi(NH - 1)
                split_wo(1)
                split_wo(2)
                split_wo(3)
                split_gate_up(1, 0, 0)

            def split_wo(u):
                act.wait_ge(s_wor[u % 2], 16 * (u // 2 + 1))
                if u == 0:
                    act.wait_ge(s_vl, NH)
                if u >= 2:
                    act.wait_ge(s_omm, 4 * (u - 1))
                act.activation(wo_hi[u % 2][:, :, :], wo_raw[u % 2][:, :, :], ACT.Copy).then_inc(s_woh, 1)

            mixer()
            ffn(0)
            latents()
            heads()
            attention()
            output_projection()
            ffn(1)
            for t in range(NT):
                act.wait_ge(s_otr, 2 * t + 2)
                act.activation(y_tok[:, t, 512:1024], ps[1 + 2 * (t % 2)][:, :], ACT.Copy).then_inc(s_oev2, 1)

        @block.vector
        def _(dve):
            steps = [0]

            def link(ins):
                steps[0] += 1
                ins.then_inc(s_dve, 1)
                dve.wait_ge(s_dve, steps[0])

            def pool_d_lo(t):
                dve.wait_ge(s_dhi, t + 1)
                tok = slice(t * P, (t + 1) * P)
                dve.tensor_tensor(lo_x[:, :, tok], pool_d_banks(t), hi_x[:, :, tok].bitcast(F),
                                  ALU.subtract).then_inc(s_dlo, 1)

            def add_y(n):
                h, k = n // KD, n % KD
                x = xT[:, k, half(h)]
                dve.wait_ge(s_py, n + 1)
                if k == 0:
                    dve.wait_ge(s_xev, NT * (h + 1))
                dve.tensor_tensor(x, x, ytmp[:, n % 2, :], ALU.add).then_inc(s_xadd, 1)

            def gains():
                dve.wait_ge(s_gT, 1)
                dve.tensor_copy(gT[:, :], ps[7][:, 0:NROW]).then_inc(s_gc, 1)
                dve.wait_ge(s_gc, 1)
                dve.tensor_tensor(bs[:, :], gT[:, ROW["b_pool"]:ROW["b_pool"] + 8],
                                  gT[:, ROW["pool_scale"]:ROW["pool_scale"] + 8], ALU.mult).then_inc(s_bs, 1)

            def evacuate_x(t):
                for b in range(2):
                    dve.wait_ge(s_xtr, 2 * t + b + 1)
                    dve.tensor_copy(xT[:, 4 * b:4 * b + 4, t * P:(t + 1) * P],
                                    ps[b][:, :].rearrange("p (k t) -> p k t", t=P)).then_inc(s_xev, 1)

            def scale_x(t):
                dve.wait_ge(s_rA, t + 1)
                dve.tensor_scalar(xtok[:, t, :], xtok[:, t, :], rms[:, t:t + 1], None, ALU.mult).then_inc(s_xs, 1)

            dve.wait_ge(s_windows, 1)
            dve.wait_ge(s_const, NCONST)
            for i in range(2):
                dve.tensor_tensor(band[:, i, :, :], band[:, i, :, :], ident[:, :].unsqueeze(1).broadcast_to([P, NW, P]),
                                  ALU.subtract).then_inc(s_band, 1)
            for t in range(NT + 2):
                if t == 4:
                    gains()
                    dve.wait_ge(s_posT, 1)
                    dve.tensor_copy(pos_f[:, :], ps[6][:, 0:NT]).then_inc(s_posc, 1)
                if t < NT:
                    evacuate_x(t)
                    scale_x(t)
                if t >= 2:
                    pool_d_lo(t - 2)
                if t == 5:
                    for k in range(KD):
                        dve.wait_ge(s_wph, k + 1)
                        dve.scalar_tensor_tensor(out=wp_lo[:, k, :], in0=wp_raw[:, k, :], scalar=gain("ln_mix_a", k),
                                                 in1=wp_hi[:, k, :].bitcast(F), op0=ALU.mult,
                                                 op1=ALU.subtract).then_inc(s_wpl, 1)
                if t >= 7:
                    for n in range(2 * (t - 7), 2 * (t - 7) + 2):
                        add_y(n)

            def square_sums(l, h):
                dve.wait_ge(s_ssm, 2 * l + h + 1)
                dve.tensor_copy(ss[:, 4 * h:4 * h + 4], ps[4 + h][:, 0:4]).then_inc(s_ss, 1)

            def low(l, h, k):
                dve.wait_ge(s_hhi, (2 * l + h) * KD + k + 1)
                dve.scalar_tensor_tensor(out=lo_x[:, k, half(h)], in0=xT[:, k, half(h)], scalar=gain(f"ln_ffn{l}", k),
                                         in1=hi_x[:, k, half(h)].bitcast(F), op0=ALU.mult,
                                         op1=ALU.subtract).then_inc(s_hlo, 1)

            def rms_diag(l, h):
                dve.wait_ge(s_r, 4 * l + h + 1)
                if h == 1:
                    dve.wait_ge(s_bc, 2 * l + 1)
                for t in range(4):
                    ins = dve.tensor_scalar(diag[:, t, :], ident[:, :], rms[:, 4 * h + t:4 * h + t + 1], None, ALU.mult)
                ins.then_inc(s_dg, 1)

            def copy_rms(l, h):
                dve.wait_ge(s_bc, 2 * l + h + 1)
                dve.tensor_copy(rbc[:, half(h)], ps[6 + h][:, :]).then_inc(s_rbc, 1)
                dve.wait_ge(s_rbc, 2 * l + h + 1)

            def split_gate_up(l, i, u):
                n = l * NF + 2 * i + u
                dve.wait_ge(s_guh, n + 1)
                dve.tensor_tensor(gu_lo[:, u, :, :], raw_gu[:, :, u * P:(u + 1) * P], gu_hi[:, u, :, :].bitcast(F),
                                  ALU.subtract).then_inc(s_gul, 1)

            def split_down(l, i, u):
                n = l * NF + 2 * i + u
                dve.wait_ge(s_wdh, n + 1)
                dve.tensor_tensor(wd_lo[:, u, :], raw_wd[:, :], wd_hi[:, u, :].bitcast(F),
                                  ALU.subtract).then_inc(s_wdl, 1)

            def a_low(l, i, u, par, h):
                n = 2 * (l * NF + 2 * i + u) + h
                dve.wait_ge(s_ahi, n + 1)
                dve.tensor_tensor(a_lo[:, par, u, half(h)], a32[:, h, :], a_hi[:, par, u, half(h)].bitcast(F),
                                  ALU.subtract).then_inc(s_alo, 1)

            def gated(l, i, u, par, before, last=False):
                for h in range(2):
                    n = 2 * (l * NF + 2 * i + u) + h
                    if isinstance(i, int) and i + u == 0:
                        square_sums(l, h)
                        rms_diag(l, h)
                        copy_rms(l, h)
                    dve.wait_ge(s_gumm, n + 1)
                    if not (isinstance(n, int) and n < 2):
                        dve.wait_ge(s_a32, n - 1)
                    dve.tensor_tensor(sil[:, h, :], ps[h][:, :], rbc[:, half(h)], ALU.mult).then_inc(s_gr1, 1)
                    if not (isinstance(n, int) and n < 2):
                        dve.wait_ge(s_alo, n - 1)
                    dve.wait_ge(s_sil, n + 1)
                    dve.tensor_tensor(a32[:, h, :], sil[:, h, :], ps[2 + h][:, :], ALU.mult).then_inc(s_a32, 1)
                    if before is not None:
                        a_low(l, *before)
                    before = (i, u, par, h)
                    if last:
                        a_low(l, *before)
                        before = None

            def evacuate_output(t):
                dve.wait_ge(s_otr, 2 * t + 1)
                dve.tensor_copy(y_tok[:, t, 0:512], ps[2 * (t % 2)][:, :]).then_inc(s_oev, 1)

            def add_down(l, i, between=None):
                g = l * NG + i
                dve.wait_ge(s_xadd, NCH * (g + 1))
                for c in range(NCH):
                    h, k = c // KD, c % KD
                    x = xT[:, k, half(h)]
                    dve.wait_ge(s_dmm, NCH * (g + 1) + c + 1)
                    dve.tensor_tensor(x, x, ps[4 + c % 4][:, :], ALU.add).then_inc(s_xadd, 1)
                    if between is not None:
                        between(h, k)

            def body(l, i, par, last):
                if not last:
                    split_gate_up(l, i + 1, 0)
                split_down(l, i, 0)
                if last:
                    split_down(l, i, 1)
                gated(l, i, 1, par, (i, 0, par, 1), last)
                if not last:
                    split_gate_up(l, i + 1, 1)
                    split_down(l, i, 1)
                if not last:
                    gated(l, i + 1, 0, 1 - par, (i, 1, par, 1))
                if last and l == 0:
                    add_down(l, i, lambda h, k: latent_weights_low(k) if h == 0 else x_low(0, k))
                elif last:
                    add_down(l, i, lambda h, k: evacuate_output(k - 3) if h == 1 and 3 <= k < 7 else None)
                else:
                    add_down(l, i)

            def ffn(l):
                for h in range(2):
                    for k in range(KD):
                        if l == 1 or h == 1:
                            low(l, h, k)
                    if h == 0:
                        if l == 0:
                            dve.wait_ge(s_wpl, KD)
                        else:
                            add_o(NCH - 2)
                            add_o(NCH - 1)
                        split_gate_up(l, 0, 1)
                gated(l, 0, 0, 0, None)
                with dve.Fori(0, NG // 2) as j:
                    body(l, 2 * j, 0, False)
                    body(l, 2 * j + 1, 1, False)
                body(l, NG - 1, 0, True)

            def x_low(h, k):
                dve.wait_ge(s_xch, KD * h + k + 1)
                dve.tensor_tensor(lo_x[:, k, half(h)], xT[:, k, half(h)], hi_x[:, k, half(h)].bitcast(F),
                                  ALU.subtract).then_inc(s_xcl, 1)

            def latent_weights_low(k):
                dve.wait_ge(s_wch, k + 1)
                for cols, name in ((slice(0, RL), "ln_kv"), (slice(RL, CW), "ln_mix_b")):
                    ins = dve.scalar_tensor_tensor(out=wc_lo[k][:, cols], in0=raw_c[:, k % 4, cols], scalar=gain(name, k),
                                                   in1=wc_hi[k][:, cols].bitcast(F), op0=ALU.mult, op1=ALU.subtract)
                ins.then_inc(s_wcl, 1)

            def x_square_sums(h):
                dve.wait_ge(s_xsm, h + 1)
                dve.tensor_copy(ss[:, 4 * h:4 * h + 4], ps[2 + h][:, 0:4]).then_inc(s_ss, 1)

            def latents():
                dve.wait_ge(s_xadd, NCH * (NG + 1))
                for k in range(KD):
                    x_low(1, k)
                x_square_sums(0)
                for t in range(NT):
                    b = 4 * (t % 2)
                    if t == 4:
                        x_square_sums(1)
                    dve.wait_ge(s_rl, t + 1)
                    if t >= 2:
                        dve.wait_ge(s_ctr, t - 1)
                    r = rms[:, t:t + 1]
                    dve.tensor_scalar(kpe[:, t, :], ps[b + 1][:, 0:ROPE], r, None, ALU.mult)
                    dve.tensor_scalar(c_tok[:, t % 2, 0:KVR], ps[b][:, 0:KVR], r, rl[:, t, 0:1], ALU.mult, ALU.mult)
                    dve.tensor_scalar(c_tok[:, t % 2, KVR:KVR + QR], ps[b + 1][:, ROPE:ROPE + QR], r, rl[:, t, 1:2],
                                      ALU.mult, ALU.mult).then_inc(s_ctok, 1)
                    if t >= 1:
                        latent_lo(t - 1)
                    if t >= 6:
                        split_unit(t - 6)
                latent_lo(NT - 1)

            def latent_lo(t):
                dve.wait_ge(s_chi, t + 1)
                tok = slice(t * P, (t + 1) * P)
                dve.tensor_tensor(cT_lo[:, :, tok], ps[6][:, :].rearrange("p (k t) -> p k t", t=P),
                                  cT_hi[:, :, tok].bitcast(F), ALU.subtract)
                dve.tensor_tensor(cqT_lo[:, :, tok], ps[7][:, 0:KQ * P].rearrange("p (k t) -> p k t", t=P),
                                  cqT_hi[:, :, tok].bitcast(F), ALU.subtract).then_inc(s_clo, 1)

            def split_unit(u):
                dve.wait_ge(s_dwh, u + 1)
                for k in range(UNITS[u][2]):
                    ins = dve.scalar_tensor_tensor(out=dw_lo[:, u % 2, k, :], in0=dw_raw[:, u % 2, k, :],
                                                   scalar=gain(unit_gain(u), k), in1=dw_hi[:, u % 2, k, :].bitcast(F),
                                                   op0=ALU.mult, op1=ALU.subtract)
                ins.then_inc(s_dwl, 1)

            def rotate_key_part():
                dve.wait_ge(s_gr, 32)
                dve.wait_ge(s_tab, 1)
                link(dve.tensor_tensor(kg[:, :, :], kpe[:, :, :],
                                       g_rope[:, 0, :].unsqueeze(1).broadcast_to([P, NT, ROPE]), ALU.mult))
                x1, x2 = kg[:, :, 0:HR], kg[:, :, HR:ROPE]
                for part, (p, q, op) in enumerate(((x1, x2, ALU.subtract), (x2, x1, ALU.add))):
                    dve.tensor_tensor(krt[:, 0, :, :], p, cos_t[:, :, :], ALU.mult)
                    link(dve.tensor_tensor(krt[:, 1, :, :], q, sin_t[:, :, :], ALU.mult))
                    for twice in range(2):
                        ins = dve.tensor_tensor(krd[:, :, twice, part * HR:(part + 1) * HR], krt[:, 0, :, :],
                                                krt[:, 1, :, :], op)
                    if part == 0:
                        link(ins)
                ins.then_inc(s_krd, 1)

            def evacuate_heads(b):
                p = b // 4
                dve.wait_ge(s_kmm, b + 1)
                dve.tensor_copy((qn, kn)[p // 4][:, 2 * (p % 4) + (b // 2) % 2, half(b % 2)],
                                ps[4 + b % 2][:, :]).then_inc(s_kev, 1)

            def head_sums(p):
                pair = slice(2 * (p % 4), 2 * (p % 4) + 2)
                rotated = sskpe[:, :].unsqueeze(1).broadcast_to([P, 2, NT]) if p >= 4 else ssqpe[:, pair, :]
                dve.wait_ge(s_kst, 4 * p + 4)
                dve.tensor_tensor((rq, rk)[p // 4][:, pair, :], ps[3 + 4 * (1 - p % 2)][:, 0:16].rearrange("p (h t) -> p h t", t=NT),
                                  rotated, ALU.add).then_inc(s_kstc, 1)

            def rotate_queries(n):
                u, c = n // 4, n % 4
                tok, hd = slice(2 * c, 2 * c + 2), slice(4 * u, 4 * u + 4)
                to = qpe[c // 2][:, 2 * (c % 2):2 * (c % 2) + 2, hd, :]
                dve.wait_ge(s_qsq, n + 1)
                dve.reduce_sum(ssqpe[:, hd, tok].rearrange("p h t -> p t h"), qsq[:, :, :, :], axis=AX.X)
                if n >= 1:
                    dve.wait_ge(s_qcs, n)
                for i in range(2):
                    ins = dve.tensor_tensor(qg[:, i, :, :], ps[n % 4][:, 256 * i:256 * i + 256].rearrange("p (h c) -> p h c", c=ROPE),
                                            g_rope[:, 1, :].unsqueeze(1).broadcast_to([P, 4, ROPE]), ALU.mult)
                ins.then_inc(s_qg, 1)
                dve.wait_ge(s_qg, n + 1)
                if n >= 1:
                    dve.wait_ge(s_qpe, n)
                dve.tensor_tensor(rt[:, 0, :, :, :], qg[:, :, :, 0:HR], table(cos_t, c), ALU.mult)
                link(dve.tensor_tensor(rt[:, 1, :, :, :], qg[:, :, :, HR:ROPE], table(sin_t, c), ALU.mult))
                dve.tensor_tensor(to[:, :, :, 0:HR], rt[:, 0, :, :, :], rt[:, 1, :, :, :], ALU.subtract)
                dve.wait_ge(s_qcs, n + 1)
                dve.tensor_tensor(to[:, :, :, HR:ROPE], rt[:, 2, :, :, :], rt[:, 3, :, :, :], ALU.add).then_inc(s_qpe, 1)

            def evacuate_values(n, t):
                dve.wait_ge(s_vmm, 8 * n + t + 1)
                dve.tensor_copy(v32[:, t, n * 2 * P:(n + 1) * 2 * P], ps[4 + t % 4][:, 0:2 * P]).then_inc(s_vev, 1)

            def heads():
                dve.wait_ge(s_gr, 32)
                dve.wait_ge(s_tab, 1)
                for n in range(4):
                    rotate_queries(n)
                for n, units in ((4, (2, 3)), (5, ()), (6, (4,)), (7, (5,))):
                    for u in units:
                        split_unit(u)
                    rotate_queries(n)
                rotate_key_part()
                split_unit(6)
                for t in range(NT):
                    evacuate_values(3, t)
                split_unit(7)
                for f in range(2):
                    dve.wait_ge(s_krtr, f + 1)
                    dve.tensor_copy(krT[:, half(f)], ps[f][:, :]).then_inc(s_krT, 1)
                dve.tensor_tensor(gkq[:, :], gain("g_k", 0), gain("g_q", 0), ALU.mult)
                for p in range(8):
                    for b in range(4 * p, 4 * p + 4):
                        evacuate_heads(b)
                        if b % 4 == 0 and p > 0:
                            head_sums(p - 1)
                        if b == 24:
                            dve.wait_ge(s_krT, 2)
                            dve.wait_ge(s_rk, 5)
                            key_diag(0, 0)
                        if b == 26:
                            scale_keys(0, 0, 2)
                            key_diag(0, 1)
                        if b == 29:
                            scale_keys(0, 1, 2)
                    if p < 6:
                        split_unit(p + 8)
                    if p == 4:
                        dve.wait_ge(s_rk, 4)
                        link(dve.tensor_scalar(rq[:, :, :], rq[:, :, :], SCALE, None, ALU.mult))
                        dve.tensor_scalar(nrq[:, :, :], rq[:, :, :], -1.0, None, ALU.mult).then_inc(s_rqs, 1)
                        values(0)
                head_sums(7)
                dve.wait_ge(s_rqs, 1)

            def values(h):
                dve.wait_ge(s_vev, NT)
                dve.wait_ge(s_veva, 3 * NT)
                dve.tensor_copy(v_hi[:, :, :], v32[:, :, bass.ds(h * P, P)]).then_inc(s_vh, 1)

            def key_diag(h, f):
                if not (isinstance(h, int) and h == 0 and f == 0):
                    dve.wait_ge(s_kbc, 2 * h + f)
                for t in range(4):
                    ins = dve.tensor_scalar(kdiag[:, t, :], ident[:, :], rk[:, h, 4 * f + t:4 * f + t + 1], None, ALU.mult)
                ins.then_inc(s_kd, 1)

            def scale_keys(h, f, bank=7):
                dve.wait_ge(s_kbc, 2 * h + f + 1)
                if not (isinstance(h, int) and h == 0 and f == 0):
                    dve.wait_ge(s_klo, 2 * h + f)
                dve.tensor_tensor(krs[:, :], krT[:, half(f)], ps[bank][:, :], ALU.mult)
                dve.scalar_tensor_tensor(out=kn[:, h, half(f)], in0=kn[:, h, half(f)], scalar=gkq[:, 0:1],
                                         in1=ps[bank][:, :], op0=ALU.mult, op1=ALU.mult).then_inc(s_kf, 1)

            def softmax_front(h, i):
                n, m, sc, slot = h * NT + i, ORDER[i], ps_scores[i % 2], slice(i % 2, i % 2 + 1)
                w = (m + 1) * P
                dve.wait_ge(s_sc, n + 1)
                dve.memset(sc[0:CHUNK, w - CHUNK:w], NEG).then_inc(s_mask, 1)
                dve.wait_ge(s_mask, n + 1)
                dve.reduce_max(mx[:, slot], sc[:, 0:w], axis=AX.X).then_inc(s_max, 1)
                dve.wait_ge(s_max, n + 1)
                dve.tensor_tensor(nb[:, slot], mx[:, slot], nrq[:, h, m:m + 1], ALU.mult).then_inc(s_nb, 1)

            def softmax_sums(h, i):
                n, slot = h * NT + i, slice(i % 2, i % 2 + 1)
                dve.wait_ge(s_exp, n + 1)
                if not (isinstance(n, int) and n < 2):
                    dve.wait_ge(s_p, n - 1)
                dve.reciprocal(rsum[:, slot], esum[:, slot]).then_inc(s_rs, 1)

            def transposed_lo(h, i):
                for c, g, count in banks_of(i):
                    part = (slice(None), slice(4 * c, 4 * c + count), slice((i % 2) * P, (i % 2 + 1) * P))
                    dve.wait_ge(s_pth, 12 * h + g)
                    dve.tensor_tensor(pt_lo[part], ps[4 + (g - 1) % 2][:, 0:count * P].rearrange("p (k q) -> p k q", q=P),
                                      pt_hi[part].bitcast(F), ALU.subtract).then_inc(s_ptl, 1)

            def head(h, first, last):
                for m in range(NT):
                    if not (first and m == 0):
                        softmax_sums(*((h, m - 1) if m >= 1 else (h - 1, 7)))
                    softmax_front(h, m)
                    if not (first and m < 2):
                        transposed_lo(*((h, m - 2) if m >= 2 else (h - 1, m + 6)))
                    if m == 2 and not first:
                        values(h)
                    if first and m == NT - 1:
                        dve.wait_ge(s_rk, 8)
                    if not last:
                        if m == 0:
                            key_diag(h + 1, 0)
                        if m == 2:
                            scale_keys(h + 1, 0)
                            key_diag(h + 1, 1)
                        if m == 4:
                            scale_keys(h + 1, 1)
                    elif m == 5:
                        split_wo(0)

            def attention():
                head(0, True, False)
                with dve.Fori(0, 3) as j:
                    for w in range(2):
                        head(2 * j + 1 + w, False, False)
                head(NH - 1, False, True)
                softmax_sums(NH - 1, 7)
                transposed_lo(NH - 1, 6)
                transposed_lo(NH - 1, 7)

            def split_wo(u):
                dve.wait_ge(s_woh, u + 1)
                dve.tensor_tensor(wo_lo[u % 2][:, :, :], wo_raw[u % 2][:, :, :], wo_hi[u % 2][:, :, :].bitcast(F),
                                  ALU.subtract).then_inc(s_wol, 1)

            def add_o(c):
                k, f = 2 * (c // 4) + c % 2, (c // 2) % 2
                x = xT[:, k, half(f)]
                dve.wait_ge(s_back[k], 16)
                dve.wait_ge(s_omm, c + 1)
                dve.tensor_tensor(x, x, ps[4 + c % 4][:, :], ALU.add).then_inc(s_ox, 1)

            def output_projection():
                split_wo(1)
                for c in range(NCH - 2):
                    add_o(c)
                    if c in (3, 7):
                        split_wo(c // 4 + 2)
                    if c == 9:
                        split_gate_up(1, 0, 0)

            split_gate_up(0, 0, 0)
            for n in range(6, NCH):
                add_y(n)
                if n >= KD:
                    low(0, 0, n - KD)
            ffn(0)
            latents()
            heads()
            attention()
            output_projection()
            ffn(1)
            for t in range(4, NT):
                evacuate_output(t)

        @block.tensor
        def _(pe):
            def three(bank, terms, first=True, last=True):
                n, m = 0, 3 * len(terms)
                for wh, wl, xh, xl in terms:
                    for w, x in ((wh, xh), (wh, xl), (wl, xh)):
                        ins = pe.matmul(bank, w, x, start=first and n == 0, stop=last and n == m - 1)
                        n += 1
                return ins

            def pool_d(t):
                pe.wait_ge(s_xs, t + 1)
                if t == 0:
                    pe.wait_ge(s_band, 2)
                if t >= 2:
                    pe.wait_ge(s_dlo, t - 1)
                banks = pool_d_banks(t)
                for k in range(KD):
                    ins = pe.matmul(banks[:, k, :], xtok[:, t, k * P:(k + 1) * P], band[:, min(t, 1), k // 2, :],
                                    start=k % 4 == 0, stop=t == 0, skip_group_check=True)
                if t >= 1:
                    for k in range(KD):
                        ins = pe.matmul(banks[:, k, 0:WMAX], xtok[:, t - 1, k * P:(k + 1) * P], band_t[:, k // 2, :],
                                        start=False, stop=True, skip_group_check=True)
                ins.then_inc(s_dmmA, 1)

            def pool_product(n):
                h, k = n // KD, n % KD
                g, cols = k // 2, slice(k % 2 * P, (k % 2 + 1) * P)
                if k == 0:
                    pe.wait_ge(s_dlo, 4 * h + 4)
                if n == 0:
                    pe.wait_ge(s_wpl, KD)
                    pe.wait_ge(s_posc, 1)
                if n >= 2:
                    pe.wait_ge(s_py, n - 1)
                three(ps[6 + n % 2][:, :], [(wp_hi[:, 2 * g + c, cols], wp_lo[:, 2 * g + c, cols],
                                             hi_x[:, 2 * g + c, half(h)], lo_x[:, 2 * g + c, half(h)])
                                            for c in range(2)]).then_inc(s_dmm, 1)

            pe.wait_ge(s_const, NCONST)
            for t in range(NT + 1):
                if t < NT:
                    pe.wait_ge(s_x[t], 16)
                    for b in range(2):
                        if t >= 1:
                            pe.wait_ge(s_xev, 2 * (t - 1) + b + 1)
                        for k in range(4):
                            ins = pe.transpose(ps[b][:, k * P:(k + 1) * P],
                                               xtok[:, t, (4 * b + k) * P:(4 * b + k + 1) * P], ident[:, :])
                        ins.then_inc(s_xtr, 1)
                if t == 3:
                    pe.wait_ge(s_posf, 1)
                    pe.transpose(ps[6][:, 0:NT], pos_row[:, :], ident[0:NT, 0:NT]).then_inc(s_posT, 1)
                    pe.wait_ge(s_g, 16 * len(g_src))
                    pe.transpose(ps[7][:, 0:NROW], grow[:, :], ident[0:NROW, 0:NROW]).then_inc(s_gT, 1)
                if t >= 1:
                    pool_d(t - 1)
                if t >= 6:
                    pool_product(2 * (t - 6))
                    pool_product(2 * (t - 6) + 1)
            for n in range(6, NCH):
                pool_product(n)

            def square_sums(l, h):
                pe.wait_ge(s_sqs, 2 * l + h + 1)
                for t in range(4):
                    ins = pe.matmul(ps[4 + h][:, t:t + 1], sq[h][:, 0, t * P:(t + 1) * P], ones[:, 0:1], start=True, stop=True)
                ins.then_inc(s_ssm, 1)

            def broadcast_rms(l, h):
                pe.wait_ge(s_dg, 2 * l + h + 1)
                for t in range(4):
                    ins = pe.matmul(ps[6 + h][:, t * P:(t + 1) * P], ones[:, :], diag[:, t, :], start=True, stop=True)
                ins.then_inc(s_bc, 1)

            def first_tile(l, h, parts):
                for k in range(KD):
                    pe.wait_ge(s_hlo, (2 * l + h) * KD + k + 1)
                    for part in parts:
                        n = 0
                        for w, x in ((gu_hi, hi_x), (gu_hi, lo_x), (gu_lo, hi_x)):
                            ins = pe.matmul(ps[2 * part + h][:, :], w[:, 0, part * KD + k, :], x[:, k, half(h)],
                                            start=k == 0 and n == 0, stop=k == KD - 1 and n == 2)
                            n += 1
                return ins

            def ffn_start(l):
                pe.wait_ge(s_gul, l * NF + 1)
                if l == 0:
                    pe.wait_ge(s_xev, 2 * NT)
                    pe.wait_ge(s_dlo, NT)
                    pe.wait_ge(s_py, NCH)
                first_tile(l, 0, (0, 1)).then_inc(s_gumm, 1)
                square_sums(l, 0)
                first_tile(l, 1, (0,))
                broadcast_rms(l, 0)
                first_tile(l, 1, (1,)).then_inc(s_gumm, 1)
                square_sums(l, 1)
                pe.wait_ge(s_gul, l * NF + 2)
                gate_half(l * NF + 1, 1, 0)
                broadcast_rms(l, 1)
                up_half(1, 0)
                gate_half(l * NF + 1, 1, 1)
                up_half(1, 1)

            def gate_up(l, i, u):
                n = l * NF + 2 * i + u
                pe.wait_ge(s_gul, n + 1)
                for h in range(2):
                    gate_half(n, u, h)
                    up_half(u, h)

            def gate_half(n, u, h):
                pe.wait_ge(s_a32, 2 * n - 1 + h)
                three(ps[h][:, :], [(gu_hi[:, u, k, :], gu_lo[:, u, k, :], hi_x[:, k, half(h)], lo_x[:, k, half(h)])
                                    for k in range(KD)])

            def up_half(u, h):
                three(ps[2 + h][:, :], [(gu_hi[:, u, KD + k, :], gu_lo[:, u, KD + k, :], hi_x[:, k, half(h)],
                                         lo_x[:, k, half(h)]) for k in range(KD)]).then_inc(s_gumm, 1)

            def down(l, i, par, last=False):
                g = l * NG + i
                pe.wait_ge(s_wdl, 2 * g + 2)
                for c in range(NCH):
                    h, k = c // KD, c % KD
                    if k == 0:
                        pe.wait_ge(s_alo, 4 * g + 3 + h)
                    pe.wait_ge(s_xadd, NCH * (g + 1) + c - 3)
                    three(ps[4 + c % 4][:, :], [(wd_hi[:, u, k * P:(k + 1) * P], wd_lo[:, u, k * P:(k + 1) * P],
                                                 a_hi[:, par, u, half(h)], a_lo[:, par, u, half(h)])
                                                for u in range(2)]).then_inc(s_dmm, 1)
                    if last and c in (KD + 3, KD + 5):
                        pe.wait_ge(s_a32, 4 * NF)
                        pe.wait_ge(s_xadd, NCH * (g + 1) + KD)
                        transpose_output(c - KD - 3)
                        transpose_output(c - KD - 2)

            def transpose_output(t):
                if t >= 2:
                    pe.wait_ge(s_oev, t - 1)
                    pe.wait_ge(s_oev2, t - 1)
                for b in range(2):
                    for k in range(4):
                        ins = pe.transpose(ps[2 * (t % 2) + b][:, k * P:(k + 1) * P],
                                           xT[:, 4 * b + k, t * P:(t + 1) * P], ident[:, :])
                    ins.then_inc(s_otr, 1)

            def ffn(l):
                ffn_start(l)
                with pe.Fori(0, NG // 2) as j:
                    for par in range(2):
                        i = 2 * j + par
                        gate_up(l, i + 1, 0)
                        down(l, i, par)
                        gate_up(l, i + 1, 1)
                down(l, NG - 1, 0, l == 1)

            def x_square_sums(h):
                pe.wait_ge(s_xadds, (KD - 1) * (h + 1))
                for t in range(4):
                    ins = pe.matmul(ps[2 + h][:, t:t + 1], csq(h, 0)[:, t * P:(t + 1) * P], ones[:, 0:1], start=True, stop=True)
                ins.then_inc(s_xsm, 1)

            def latents():
                for t in range(NT):
                    b, tok = 4 * (t % 2), slice(t * P, (t + 1) * P)
                    if t == 1:
                        pe.wait_ge(s_xadd, NCH * (NG + 1))
                    if t == 4:
                        pe.wait_ge(s_xcl, 2 * KD)
                    if t >= 2:
                        pe.wait_ge(s_ctok, t - 1)
                    for k in range(KD):
                        if t == 0:
                            pe.wait_ge(s_wcl, k + 1)
                            pe.wait_ge(s_xcl, k + 1)
                        n = 0
                        for x, w in ((hi_x, wc_hi), (hi_x, wc_lo), (lo_x, wc_hi)):
                            first, last = k == 0 and n == 0, k == KD - 1 and n == 2
                            pe.matmul(ps[b][:, 0:KVR], x[:, k, tok], w[k][:, 0:KVR], start=first, stop=last)
                            ins = pe.matmul(ps[b + 1][:, 0:ROPE + QR], x[:, k, tok], w[k][:, KVR:CW], start=first, stop=last)
                            n += 1
                    ins.then_inc(s_cmm, 1)
                    if t == 0:
                        x_square_sums(0)
                    if t == 3:
                        x_square_sums(1)
                    if t >= 1:
                        transpose_latents(t - 1)

            def transpose_latents(t):
                pe.wait_ge(s_ctok, t + 1)
                if t >= 1:
                    pe.wait_ge(s_clo, t)
                for k in range(KC):
                    pe.transpose(ps[6][:, k * P:(k + 1) * P], c_tok[:, t % 2, k * P:(k + 1) * P], ident[:, :])
                for k in range(KQ):
                    ins = pe.transpose(ps[7][:, k * P:(k + 1) * P], c_tok[:, t % 2, KVR + k * P:KVR + (k + 1) * P], ident[:, :])
                ins.then_inc(s_ctr, 1)

            def rotated_queries(n):
                u, c = 2 * (n // 4), n % 4
                pe.wait_ge(s_dwl, u + 1)
                pe.wait_ge(s_clo, 2 * c + 2)
                if n >= 4:
                    pe.wait_ge(s_qg, n - 3)
                else:
                    pe.wait_ge(s_ss, 4)
                for i in range(2):
                    tok = slice((2 * c + i) * P, (2 * c + i + 1) * P)
                    ins = three(ps[n % 4][:, 2 * P * i:2 * P * (i + 1)],
                                [(cqT_hi[:, k, tok], cqT_lo[:, k, tok], dw_hi[:, 0, k, :], dw_lo[:, 0, k, :])
                                 for k in range(KQ)])
                ins.then_inc(s_qrmm, 1)

            def value_products(n, t):
                u = (1, 3, 4, 5)[n]
                tok = slice(t * P, (t + 1) * P)
                pe.wait_ge(s_dwl, u + 1)
                pe.wait_ge(s_clo, NT)
                before = 8 * n + t - 4
                if before >= 3 * NT:
                    pe.wait_ge(s_vev, before - 3 * NT + 1)
                elif before >= 0:
                    pe.wait_ge(s_veva, before + 1)
                three(ps[4 + t % 4][:, 0:2 * P], [(cT_hi[:, k, tok], cT_lo[:, k, tok], dw_hi[:, u % 2, k, :],
                                                   dw_lo[:, u % 2, k, :]) for k in range(KC)]).then_inc(s_vmm, 1)

            def head_product(b):
                p, hh, f = b // 4, (b // 2) % 2, b % 2
                nk, x_hi, x_lo = (KQ, cqT_hi, cqT_lo) if p < 4 else (KC, cT_hi, cT_lo)
                if b % 4 == 0:
                    pe.wait_ge(s_dwl, p + 7)
                if b >= 2:
                    pe.wait_ge(s_kev, b - 1)
                cols = slice(hh * P, (hh + 1) * P)
                three(ps[4 + b % 2][:, :], [(dw_hi[:, p % 2, k, cols], dw_lo[:, p % 2, k, cols], x_hi[:, k, half(f)],
                                             x_lo[:, k, half(f)]) for k in range(nk)]).then_inc(s_kmm, 1)

            def head_square_sums(b):
                p = b // 4
                pe.wait_ge(s_ksq, b + 1)
                if b % 4 == 0 and p >= 2:
                    pe.wait_ge(s_kstc, p - 1)
                bank = ps[3 + 4 * (1 - p % 2)]
                for t in range(4):
                    col = 4 * (b % 4) + t
                    ins = pe.matmul(bank[:, col:col + 1], dsq[:, b % 2, t * P:(t + 1) * P], ones[:, 0:1], start=True, stop=True)
                ins.then_inc(s_kst, 1)

            def heads():
                for n in range(3):
                    rotated_queries(n)
                transpose_latents(NT - 1)
                for t in range(4):
                    value_products(0, t)
                rotated_queries(3)
                for t in range(4, NT):
                    value_products(0, t)
                for c in range(4):
                    rotated_queries(4 + c)
                for n in range(1, 4):
                    for t in range(NT):
                        value_products(n, t)
                pe.wait_ge(s_krd, 1)
                pe.wait_ge(s_qg, 8)
                for f in range(2):
                    for t in range(4):
                        ins = pe.transpose(ps[f][:, t * P:(t + 1) * P],
                                           krd[:, 4 * f + t, :, :].rearrange("p a c -> p (a c)"), ident[:, :])
                    ins.then_inc(s_krtr, 1)
                pe.wait_ge(s_vev, NT)
                for b in range(32):
                    head_product(b)
                    if b > 0:
                        head_square_sums(b - 1)
                    if b == 21:
                        query_part(0, 0, 0)
                        query_part(0, 1, 1)
                    if b in (25, 28):
                        key_rms(0, (b - 25) // 3, 2)
                head_square_sums(31)

            def key_rms(h, f, bank=7):
                pe.wait_ge(s_kd, 2 * h + f + 1)
                if f == 1:
                    pe.wait_ge(s_kf, 2 * h + 1)
                elif not (isinstance(h, int) and h == 0):
                    pe.wait_ge(s_qs, 2 * h)
                for t in range(4):
                    ins = pe.matmul(ps[bank][:, t * P:(t + 1) * P], ones[:, :], kdiag[:, t, :], start=True, stop=True)
                ins.then_inc(s_kbc, 1)

            def query_part(h, f, bank=7):
                pe.wait_ge(s_qhl, h + 1)
                if bank == 7:
                    pe.wait_ge(s_kf, 2 * h + 2)
                    if f == 1:
                        pe.wait_ge(s_qs, 2 * h + 1)
                for t in range(4):
                    ins = pe.transpose(ps[bank][:, t * P:(t + 1) * P],
                                       qhl[:, 4 * f + t, :, :].rearrange("p a c -> p (a c)").bitcast(F), ident[:, :])
                ins.then_inc(s_qtr, 1)

            def scores(h, u, i):
                n, m = h * NT + i, ORDER[i]
                w, q = (m + 1) * P, slice(m * P, (m + 1) * P)
                if i == 0:
                    pe.wait_ge(s_klo, 2 * h + 2)
                    pe.wait_ge(s_ql, h + 1)
                    pe.wait_ge(s_qs, 2 * h + 2)
                if not (isinstance(n, int) and n < 2):
                    pe.wait_ge(s_exp, n - 1)
                for c in range(m // 4 + 1):
                    keys = slice(c * 512, min(w, (c + 1) * 512))
                    terms = ((qhi, khi[u][:, keys]), (qhi, klo[:, h, keys]), (qlo, khi[u][:, keys]),
                             (qs, kr1[u][:, keys]), (qs, kr2[u][:, keys]))
                    for term, (query, key) in enumerate(terms):
                        ins = pe.matmul(ps_scores[i % 2][:, keys], query[u][:, q], key, start=term == 0, stop=term == 4)
                ins.then_inc(s_sc, 1)

            def transposes(h, i):
                pe.wait_ge(s_p, h * NT + i + 1)
                for c, g, count in banks_of(i):
                    if not (isinstance(h, int) and h == 0 and g <= 2):
                        pe.wait_ge(s_ptl, 12 * h + g - 2)
                    for k in range(count):
                        ins = pe.transpose(ps[4 + (g - 1) % 2][:, k * P:(k + 1) * P],
                                           e32[:, i % 3, (4 * c + k) * P:(4 * c + k + 1) * P], ident[:, :])
                    ins.then_inc(s_ptr, 1)

            def weighted_values(h, j):
                pe.wait_ge(s_ptl, 12 * h + TR[2 * j + 1])
                if j == 0:
                    pe.wait_ge(s_vl, h + 1)
                if not (isinstance(h, int) and h == 0 and j == 0):
                    pe.wait_ge(s_o, 4 * h + j)
                last = ORDER[2 * j + 1]
                for k in range(last + 1):
                    q = slice(P if k == last else 0, 2 * P)
                    for i, (v, pt) in enumerate(((v_hi, pt_hi), (v_hi, pt_lo), (v_lo, pt_hi))):
                        ins = pe.matmul(ps[6][:, q], v[:, k, :], pt[:, k, q], start=k == 0 and i == 0,
                                        stop=k == last and i == 2)
                ins.then_inc(s_pv, 1)

            def head(h, u, first, last):
                for m in range(NT):
                    scores(h, u, m)
                    if m in (0, 2) and not first:
                        weighted_values(h - 1, 2 + m // 2)
                    if m in (4, 6):
                        weighted_values(h, m // 2 - 2)
                    if not (first and m < 2):
                        transposes(*((h, m - 2) if m >= 2 else (h - 1, m + 6)))
                    if not last:
                        if m in (1, 3):
                            key_rms(h + 1, m // 2)
                        if m in (5, 6):
                            query_part(h + 1, m - 5)

            def attention():
                head(0, 0, True, False)
                with pe.Fori(0, 3) as j:
                    for w in range(2):
                        head(2 * j + 1 + w, 1 - w, False, False)
                head(NH - 1, 1, False, True)
                weighted_values(NH - 1, 2)
                transposes(NH - 1, 6)
                transposes(NH - 1, 7)
                weighted_values(NH - 1, 3)

            def output_projection():
                pe.wait_ge(s_ol, NH - 1)
                for c in range(NCH):
                    u, f, dt = c // 4, (c // 2) % 2, c % 2
                    if c % 4 == 0:
                        pe.wait_ge(s_wol, u + 1)
                    if c >= 4:
                        pe.wait_ge(s_ox, c - 3)
                    cols = slice(dt * P, (dt + 1) * P)
                    for k in range(NH):
                        if c == 0 and k == NH - 1:
                            pe.wait_ge(s_ol, NH)
                        ins = three(ps[4 + c % 4][:, :], [(wo_hi[u % 2][:, k, cols], wo_lo[u % 2][:, k, cols],
                                                           hi_x[:, k, half(f)], lo_x[:, k, half(f)])],
                                    first=k == 0, last=k == NH - 1)
                    ins.then_inc(s_omm, 1)

            ffn(0)
            latents()
            heads()
            attention()
            output_projection()
            ffn(1)
            pe.wait_ge(s_xadd, NCH * (1 + 2 * NG))
            for t in range(4, NT):
                transpose_output(t)


_INS = ["x", "positions", "ln_mix_a", "w_pool", "b_pool", "pool_scale", "ln_ffn", "w_gate", "w_up", "w_down",
        "ln_kv", "w_dkv", "g_kv_latent", "w_uk", "w_uv", "g_k", "ln_mix_b", "w_dq", "g_q_latent", "w_uq", "g_q", "w_o"]


def kernel(**inputs):
    import concourse.bacc as bacc
    from concourse.bass_utils import run_bass_kernel_spmd

    nc = bacc.Bacc("TRN2", target_bir_lowering=False, num_devices=1, dynamic_dma_scratch_size=1024)
    arrays, aps = {}, {}
    for name in _INS:
        v = np.ascontiguousarray(inputs[name])
        arrays[f"in_{name}"] = v
        aps[name] = nc.dram_tensor(f"in_{name}", v.shape, mybir.dt.from_np(v.dtype), kind="ExternalInput").ap()
    shape = inputs["x"].shape
    out = nc.dram_tensor("out_x", shape, mybir.dt.float32, kind="ExternalOutput").ap()
    build_trunk(nc, aps, out)
    r = run_bass_kernel_spmd(nc, [arrays], core_ids=[0])
    return r.results[0]["out_x"]
```
